# Optimizing a Trainium2 kernel written in Bass

```python
import jax, jax.numpy as jnp
from jax import lax
import numpy as np
import math

D_MODEL = 1024
BATCH = 1
SEQ = 512
DEPTH = 1

N_HEADS = 16
HEAD_DIM = 64
N_KV = 4
GROUP = N_HEADS // N_KV
ROPE_DIM = HEAD_DIM // 4
ROPE_THETA = 500000.0
CMP_BLOCK = 32
CMP_STRIDE = 16
CMP_HIDDEN = 4 * HEAD_DIM
SEL_BLOCK = 64
SEL_TOPK = 16
WINDOW = 512
Q_BLOCK = 128
CONV_DIM = D_MODEL
CONV_WIDTH = 31
D_FF = ((8 * D_MODEL // 3 + 255) // 256) * 256
EPS = 1e-6


SPLIT_SIZES = [N_HEADS * HEAD_DIM] + [N_KV * HEAD_DIM] * 6 + [3 * N_HEADS, CONV_DIM, CONV_DIM, D_MODEL, D_MODEL]
IN_COLS = sum(SPLIT_SIZES)

def rms_norm(x, g):
    xf = x.astype(jnp.float32)
    y = xf * lax.rsqrt(jnp.mean(xf * xf, axis=-1, keepdims=True) + EPS)
    return (y * g.astype(jnp.float32)).astype(x.dtype)

def rope_tables(positions, dtype):
    inv = ROPE_THETA ** (-jnp.arange(0, ROPE_DIM, 2, dtype=jnp.float32) / ROPE_DIM)
    ang = positions.astype(jnp.float32)[..., None] * inv
    return jnp.cos(ang).astype(dtype), jnp.sin(ang).astype(dtype)

def apply_partial_rope(t, cos, sin):
    half = ROPE_DIM // 2
    c = cos[:, :, None, :]
    s = sin[:, :, None, :]
    t1 = t[..., :half]
    t2 = t[..., half:ROPE_DIM]
    return jnp.concatenate([t1 * c - t2 * s, t2 * c + t1 * s, t[..., ROPE_DIM:]], axis=-1)

def masked_softmax(s, mask):
    s = jnp.where(mask, s, -jnp.inf)
    m = jnp.max(s, axis=-1, keepdims=True)
    m = jnp.where(jnp.isfinite(m), m, 0.0)
    e = jnp.where(mask, jnp.exp(s - m), 0.0)
    d = jnp.sum(e, axis=-1, keepdims=True)
    return e / jnp.where(d > 0, d, 1.0)

def compress_blocks(t, pos_emb, w1, w2):
    B, G, S, Dh = t.shape
    chunks = t.reshape(B, G, S // CMP_STRIDE, CMP_STRIDE, Dh)
    blocks = jnp.concatenate([chunks[:, :, :-1], chunks[:, :, 1:]], axis=3)
    blocks = (blocks + pos_emb).reshape(B, G, -1, CMP_BLOCK * Dh)
    return jax.nn.silu(blocks @ w1) @ w2

def gather_sel_blocks(t, idx):
    B, G, S, Dh = t.shape
    Qn, K = idx.shape[2], idx.shape[3]
    tb = t.reshape(B, G, S // SEL_BLOCK, SEL_BLOCK * Dh)
    g = jax.vmap(jax.vmap(lambda a, i: a[i]))(tb, idx.reshape(B, G, Qn * K))
    return g.reshape(B, G, Qn, K * SEL_BLOCK, Dh)

def nsa_attention(q, k_c, v_c, k_s, v_s, k_w, v_w, gates):
    B, G, R, S, Dh = q.shape
    dt = q.dtype
    scale = HEAD_DIM ** -0.5
    n_cmp = k_c.shape[2]
    n_sel = S // SEL_BLOCK
    top_k = min(SEL_TOPK, n_sel)
    c_end = jnp.arange(n_cmp) * CMP_STRIDE + CMP_BLOCK - 1
    ks = jnp.arange(n_cmp)[:, None] * CMP_STRIDE
    bs = jnp.arange(n_sel)[None, :] * SEL_BLOCK
    overlap = (jnp.clip(jnp.minimum(ks + CMP_BLOCK, bs + SEL_BLOCK) - jnp.maximum(ks, bs), 0)
               .astype(jnp.float32) / CMP_STRIDE)
    k_w_pad = jnp.pad(k_w, ((0, 0), (0, 0), (WINDOW, 0), (0, 0)))
    v_w_pad = jnp.pad(v_w, ((0, 0), (0, 0), (WINDOW, 0), (0, 0)))
    sel_off = jnp.arange(SEL_BLOCK)
    j_all = jnp.arange(n_sel)

    def one_block(i):
        t0 = i * Q_BLOCK
        qb = lax.dynamic_slice_in_dim(q, t0, Q_BLOCK, axis=3)
        gb = lax.dynamic_slice_in_dim(gates, t0, Q_BLOCK, axis=3)
        tpos = t0 + jnp.arange(Q_BLOCK)
        s_c = jnp.einsum('bgrqd,bgnd->bgrqn', qb, k_c).astype(jnp.float32) * scale
        p_c = masked_softmax(s_c, c_end[None, :] <= tpos[:, None])
        o_c = jnp.einsum('bgrqn,bgnd->bgrqd', p_c.astype(dt), v_c)
        imp = jnp.einsum('bgrqn,nj->bgqj', p_c, overlap)
        qblk = tpos // SEL_BLOCK
        forced = (j_all[None, :] == 0) | (j_all[None, :] == qblk[:, None]) | (j_all[None, :] == qblk[:, None] - 1)
        causal = j_all[None, :] <= qblk[:, None]
        score = jnp.where(forced, jnp.inf, jnp.where(causal, imp, -jnp.inf))
        vals, idx = lax.top_k(score, top_k)
        ks_g = gather_sel_blocks(k_s, idx)
        vs_g = gather_sel_blocks(v_s, idx)
        tok = idx[..., None] * SEL_BLOCK + sel_off
        m_s = ((vals != -jnp.inf)[..., None] & (tok <= tpos[:, None, None])).reshape(B, G, Q_BLOCK, top_k * SEL_BLOCK)
        s_s = jnp.einsum('bgrqd,bgqkd->bgrqk', qb, ks_g).astype(jnp.float32) * scale
        p_s = masked_softmax(s_s, m_s[:, :, None])
        o_s = jnp.einsum('bgrqk,bgqkd->bgrqd', p_s.astype(dt), vs_g)
        kw = lax.dynamic_slice_in_dim(k_w_pad, t0, WINDOW + Q_BLOCK, axis=2)
        vw = lax.dynamic_slice_in_dim(v_w_pad, t0, WINDOW + Q_BLOCK, axis=2)
        kpos = t0 - WINDOW + jnp.arange(WINDOW + Q_BLOCK)
        m_w = (kpos[None, :] <= tpos[:, None]) & (kpos[None, :] > tpos[:, None] - WINDOW) & (kpos[None, :] >= 0)
        s_w = jnp.einsum('bgrqd,bgkd->bgrqk', qb, kw).astype(jnp.float32) * scale
        p_w = masked_softmax(s_w, m_w)
        o_w = jnp.einsum('bgrqk,bgkd->bgrqd', p_w.astype(dt), vw)
        return gb[..., 0:1] * o_c + gb[..., 1:2] * o_s + gb[..., 2:3] * o_w

    out = lax.map(one_block, jnp.arange(S // Q_BLOCK))
    return out.transpose(1, 0, 4, 2, 3, 5).reshape(B, S, G * R * Dh)

def conformer_conv(u_a, u_b, conv_w, conv_b, ln_g, ln_b, w_o, b_o):
    z = u_a * jax.nn.sigmoid(u_b)
    zp = jnp.pad(z, ((0, 0), (CONV_WIDTH - 1, 0), (0, 0)))
    z = lax.conv_general_dilated(zp, conv_w, window_strides=(1,), padding='VALID',
                                 dimension_numbers=('NWC', 'WIO', 'NWC'),
                                 feature_group_count=CONV_DIM) + conv_b
    zf = z.astype(jnp.float32)
    mu = jnp.mean(zf, axis=-1, keepdims=True)
    var = jnp.mean(jnp.square(zf - mu), axis=-1, keepdims=True)
    zn = ((zf - mu) * lax.rsqrt(var + EPS) * ln_g.astype(jnp.float32) + ln_b.astype(jnp.float32)).astype(z.dtype)
    return jax.nn.silu(zn) @ w_o + b_o

def first_inputs(seed: int = 0) -> dict:
    key = jax.random.key(seed)
    ks = jax.random.split(key, 24)
    f32 = jnp.float32
    nrm = lambda k, shape, s: jax.random.normal(k, shape, f32) * s
    d = D_MODEL
    return {
        'x': jax.random.normal(ks[0], (BATCH, SEQ, d), f32),
        'positions': jnp.broadcast_to(jnp.arange(SEQ, dtype=jnp.int32), (BATCH, SEQ)),
        'norm_mix_g': 1.0 + nrm(ks[1], (d,), 0.01),
        'w_in': nrm(ks[2], (d, IN_COLS), d ** -0.5),
        'cmp_k_pos': nrm(ks[3], (CMP_BLOCK, HEAD_DIM), 0.02),
        'cmp_k_w1': nrm(ks[4], (CMP_BLOCK * HEAD_DIM, CMP_HIDDEN), (CMP_BLOCK * HEAD_DIM) ** -0.5),
        'cmp_k_w2': nrm(ks[5], (CMP_HIDDEN, HEAD_DIM), CMP_HIDDEN ** -0.5),
        'cmp_v_pos': nrm(ks[6], (CMP_BLOCK, HEAD_DIM), 0.02),
        'cmp_v_w1': nrm(ks[7], (CMP_BLOCK * HEAD_DIM, CMP_HIDDEN), (CMP_BLOCK * HEAD_DIM) ** -0.5),
        'cmp_v_w2': nrm(ks[8], (CMP_HIDDEN, HEAD_DIM), CMP_HIDDEN ** -0.5),
        'conv_w': nrm(ks[9], (CONV_WIDTH, 1, CONV_DIM), CONV_WIDTH ** -0.5),
        'conv_b': nrm(ks[10], (CONV_DIM,), 0.01),
        'conv_norm_g': 1.0 + nrm(ks[11], (CONV_DIM,), 0.01),
        'conv_norm_b': nrm(ks[12], (CONV_DIM,), 0.01),
        'w_conv_out': nrm(ks[13], (CONV_DIM, d), CONV_DIM ** -0.5),
        'b_conv_out': nrm(ks[14], (d,), 0.01),
        'w_out': nrm(ks[15], (d, d), d ** -0.5),
        'norm_ffn_g': 1.0 + nrm(ks[16], (d,), 0.01),
        'w_ffn_gate': nrm(ks[17], (d, D_FF), d ** -0.5),
        'w_ffn_up': nrm(ks[18], (d, D_FF), d ** -0.5),
        'w_ffn_down': nrm(ks[19], (D_FF, d), D_FF ** -0.5),
        'norm_final_g': 1.0 + nrm(ks[20], (d,), 0.01),
    }

def first_block(x, positions, norm_mix_g, w_in, cmp_k_pos, cmp_k_w1, cmp_k_w2, cmp_v_pos, cmp_v_w1, cmp_v_w2,
              conv_w, conv_b, conv_norm_g, conv_norm_b, w_conv_out, b_conv_out, w_out,
              norm_ffn_g, w_ffn_gate, w_ffn_up, w_ffn_down, norm_final_g):
    B, S, _ = x.shape
    cos, sin = rope_tables(positions, x.dtype)
    split_idx = [int(v) for v in np.cumsum(SPLIT_SIZES)[:-1]]
    for _layer in range(DEPTH):
        h = rms_norm(x, norm_mix_g)
        parts = jnp.split(h @ w_in, split_idx, axis=-1)
        (q, kc, vc, ks_, vs_, kw, vw, g_nsa, u_a, u_b, g_attn, g_conv) = parts
        q = apply_partial_rope(q.reshape(B, S, N_HEADS, HEAD_DIM), cos, sin)
        q = q.reshape(B, S, N_KV, GROUP, HEAD_DIM).transpose(0, 2, 3, 1, 4)
        rk = lambda t: apply_partial_rope(t.reshape(B, S, N_KV, HEAD_DIM), cos, sin).transpose(0, 2, 1, 3)
        rv = lambda t: t.reshape(B, S, N_KV, HEAD_DIM).transpose(0, 2, 1, 3)
        k_c = compress_blocks(rk(kc), cmp_k_pos, cmp_k_w1, cmp_k_w2)
        v_c = compress_blocks(rv(vc), cmp_v_pos, cmp_v_w1, cmp_v_w2)
        gates = jax.nn.sigmoid(g_nsa).reshape(B, S, 3, N_KV, GROUP).transpose(0, 3, 4, 1, 2)
        attn = nsa_attention(q, k_c, v_c, rk(ks_), rv(vs_), rk(kw), rv(vw), gates)
        conv = conformer_conv(u_a, u_b, conv_w, conv_b, conv_norm_g, conv_norm_b, w_conv_out, b_conv_out)
        merged = jax.nn.sigmoid(g_attn) * attn + jax.nn.sigmoid(g_conv) * conv
        x = x + merged @ w_out
        h = rms_norm(x, norm_ffn_g)
        x = x + (jax.nn.silu(h @ w_ffn_gate) * (h @ w_ffn_up)) @ w_ffn_down
    return rms_norm(x, norm_final_g)


_first_inputs = first_inputs


def first_inputs(seed=0):
    import zlib

    import numpy as np

    out = dict(_first_inputs(seed))
    spreads = {}
    factors = {'norm_mix_g': 8.0,
     'cmp_k_pos': 8.0,
     'cmp_v_pos': 8.0,
     'conv_b': 8.0,
     'conv_norm_g': 8.0,
     'conv_norm_b': 8.0,
     'b_conv_out': 8.0,
     'norm_ffn_g': 8.0,
     'norm_final_g': 5.895}
    for name, (base, spread) in spreads.items():
        noise = np.random.default_rng([zlib.crc32(name.encode()), seed]).standard_normal(out[name].shape)
        drawn = base * np.exp(spread * noise) if base else spread * noise
        out[name] = __import__('jax').numpy.asarray(drawn.astype(out[name].dtype))
    for name, factor in factors.items():
        out[name] = (out[name] * factor).astype(out[name].dtype)
    return out


_narrow_inputs = first_inputs


def first_inputs(seed=0):

    out = dict(_narrow_inputs(seed))
    wider = {'cmp_v_pos': 7.01,
     'conv_b': 5.08,
     'conv_norm_g': 7.95,
     'conv_norm_b': 8.09,
     'b_conv_out': 5.78,
     'norm_ffn_g': 4.56,
     'norm_final_g': 6.64}
    for name, times in wider.items():
        mean = out[name].mean()
        out[name] = (mean + times * (out[name] - mean)).astype(out[name].dtype)
    return out


POOL_WINDOWS = (2, 4, 8, 16)
N_POOL_GROUPS = 4
POOL_WIDTH = D_MODEL // 2
POOL_GROUP = POOL_WIDTH // N_POOL_GROUPS
POOL_OUT_GROUP = D_MODEL // N_POOL_GROUPS
DN_HEADS = 8
DN_HEAD_DIM = 128
DN_WIDTH = DN_HEADS * DN_HEAD_DIM
CONV_K = 4
CHUNK = 64
D_FF_2 = 4 * D_MODEL
PLE_DIM = 256
LN_EPS = 1e-5
RMS_EPS = 1e-6
L2_EPS = 1e-6
DEEPNORM_ALPHA = (2.0 * DEPTH) ** 0.25
DEEPNORM_BETA = (8.0 * DEPTH) ** -0.25
QKV_WIDTH = 3 * DN_WIDTH
IN_WIDTH = POOL_WIDTH + QKV_WIDTH + DN_WIDTH + DN_HEADS + DN_HEADS + 2 * D_MODEL
SPLIT_POINTS = (
    POOL_WIDTH,
    POOL_WIDTH + QKV_WIDTH,
    POOL_WIDTH + QKV_WIDTH + DN_WIDTH,
    POOL_WIDTH + QKV_WIDTH + DN_WIDTH + DN_HEADS,
    POOL_WIDTH + QKV_WIDTH + DN_WIDTH + 2 * DN_HEADS,
    POOL_WIDTH + QKV_WIDTH + DN_WIDTH + 2 * DN_HEADS + D_MODEL,
)


def _layer_norm(x, g, b):
    xf = x.astype(jnp.float32)
    mu = jnp.mean(xf, axis=-1, keepdims=True)
    var = jnp.mean(jnp.square(xf - mu), axis=-1, keepdims=True)
    y = (xf - mu) * lax.rsqrt(var + LN_EPS) * g.astype(jnp.float32) + b.astype(jnp.float32)
    return y.astype(x.dtype)

def _multiscale_pool(u, pool_w, pool_scale):
    bsz, seq, _ = u.shape
    ug = u.astype(jnp.float32).reshape(bsz, seq, N_POOL_GROUPS, POOL_GROUP)
    cs = jnp.cumsum(ug, axis=1)
    outs = []
    for gi, w in enumerate(POOL_WINDOWS):
        c = cs[:, :, gi]
        prev = jnp.pad(c, ((0, 0), (w, 0), (0, 0)))[:, :seq]
        cnt = jnp.minimum(jnp.arange(1, seq + 1), w).astype(jnp.float32)[None, :, None]
        outs.append((c - prev) / cnt - ug[:, :, gi])
    d = jnp.stack(outs, axis=2).astype(u.dtype)
    y = jnp.einsum('bsgc,gcd->bsgd', d, pool_w).reshape(bsz, seq, D_MODEL)
    return y * pool_scale

def _causal_depthwise_conv_silu(x, w):
    ch = x.shape[-1]
    y = lax.conv_general_dilated(
        x, w[:, None, :].astype(x.dtype), window_strides=(1,),
        padding=((CONV_K - 1, 0),), dimension_numbers=('NWC', 'WIO', 'NWC'),
        feature_group_count=ch)
    return jax.nn.silu(y)

def _l2norm(t):
    return t * lax.rsqrt(jnp.sum(jnp.square(t), axis=-1, keepdims=True) + L2_EPS)

def _chunk_gated_delta_rule(q, k, v, beta, g):
    bsz, seq, nh, dk = q.shape
    dv = v.shape[-1]
    n_chunks = seq // CHUNK

    def to_chunks(t):
        t = t.reshape((bsz, n_chunks, CHUNK, nh) + t.shape[3:])
        return jnp.moveaxis(t, 3, 2)

    q, k, v, beta, g = (to_chunks(t) for t in (q, k, v, beta, g))
    gc = jnp.cumsum(g, axis=-1)
    idx = jnp.arange(CHUNK)
    incl = idx[:, None] >= idx[None, :]
    strict = idx[:, None] > idx[None, :]
    decay = jnp.exp(jnp.where(incl, gc[..., :, None] - gc[..., None, :], -jnp.inf))
    kb = k * beta[..., None]
    m = jnp.where(strict, jnp.einsum('bnhid,bnhjd->bnhij', kb, k) * decay, 0.0)
    a = m + jnp.eye(CHUNK, dtype=m.dtype)
    rhs = jnp.concatenate([v * beta[..., None], kb * jnp.exp(gc)[..., None]], axis=-1)
    sol = lax.linalg.triangular_solve(a, rhs, left_side=True, lower=True, unit_diagonal=True)
    u, w = sol[..., :dv], sol[..., dv:]
    attn = jnp.einsum('bnhid,bnhjd->bnhij', q, k) * decay
    qg = q * jnp.exp(gc)[..., None]
    gl = gc[..., -1]
    kg = k * jnp.exp(gl[..., None] - gc)[..., None]
    xs = tuple(jnp.moveaxis(t, 1, 0) for t in (qg, kg, u, w, attn, gl))

    def step(state, inp):
        qg_n, kg_n, u_n, w_n, attn_n, gl_n = inp
        v_new = u_n - jnp.einsum('bhcd,bhde->bhce', w_n, state)
        o = jnp.einsum('bhcd,bhde->bhce', qg_n, state) + jnp.einsum('bhij,bhje->bhie', attn_n, v_new)
        state = state * jnp.exp(gl_n)[..., None, None] + jnp.einsum('bhcd,bhce->bhde', kg_n, v_new)
        return state, o

    s0 = jnp.zeros((bsz, nh, dk, dv), jnp.float32)
    _, o = lax.scan(step, s0, xs)
    o = jnp.moveaxis(o, 0, 1)
    return jnp.moveaxis(o, 2, 3).reshape(bsz, seq, nh, dv)

def _gated_deltanet(qkv, z, beta_raw, a_raw, conv_w, a_log, dt_bias, o_norm_w):
    bsz, seq, _ = qkv.shape
    qkv = _causal_depthwise_conv_silu(qkv, conv_w)
    q, k, v = jnp.split(qkv.astype(jnp.float32), 3, axis=-1)
    shp = (bsz, seq, DN_HEADS, DN_HEAD_DIM)
    q = _l2norm(q.reshape(shp)) * (DN_HEAD_DIM ** -0.5)
    k = _l2norm(k.reshape(shp))
    v = v.reshape(shp)
    beta = jax.nn.sigmoid(beta_raw.astype(jnp.float32))
    g = -jnp.exp(a_log.astype(jnp.float32)) * jax.nn.softplus(
        a_raw.astype(jnp.float32) + dt_bias.astype(jnp.float32))
    o = _chunk_gated_delta_rule(q, k, v, beta, g)
    o = o * lax.rsqrt(jnp.mean(jnp.square(o), axis=-1, keepdims=True) + RMS_EPS)
    o = o * o_norm_w.astype(jnp.float32) * jax.nn.silu(z.astype(jnp.float32).reshape(shp))
    return o.reshape(bsz, seq, DN_WIDTH).astype(qkv.dtype)

def second_inputs(seed: int = 0) -> dict:
    key = jax.random.key(seed)
    ks = jax.random.split(key, 24)
    f32 = jnp.float32
    nrm = lambda k, shape, s: jax.random.normal(k, shape, f32) * s
    x = jax.random.normal(ks[0], (BATCH, SEQ, D_MODEL), f32)
    p = jax.random.normal(ks[1], (DEPTH, BATCH, SEQ, PLE_DIM), f32)
    ln_in_g = 1.0 + nrm(ks[2], (D_MODEL,), 0.02)
    ln_in_b = nrm(ks[3], (D_MODEL,), 0.02)
    s_in = D_MODEL ** -0.5
    w_pool_qk = nrm(ks[4], (DEPTH, D_MODEL, POOL_WIDTH + 2 * DN_WIDTH), s_in)
    w_v = nrm(ks[5], (DEPTH, D_MODEL, DN_WIDTH), s_in * DEEPNORM_BETA)
    w_rest = nrm(ks[6], (DEPTH, D_MODEL, IN_WIDTH - POOL_WIDTH - QKV_WIDTH), s_in)
    w_in = jnp.concatenate([w_pool_qk, w_v, w_rest], axis=-1)
    pool_w = nrm(ks[7], (DEPTH, N_POOL_GROUPS, POOL_GROUP, POOL_OUT_GROUP), POOL_GROUP ** -0.5)
    pool_scale = 1.0 + nrm(ks[8], (DEPTH, D_MODEL), 0.02)
    conv_w = nrm(ks[9], (DEPTH, CONV_K, QKV_WIDTH), CONV_K ** -0.5)
    a_log = jnp.log(jax.random.uniform(ks[10], (DEPTH, DN_HEADS), f32, 1.0, 16.0))
    dt = jnp.exp(jax.random.uniform(ks[11], (DEPTH, DN_HEADS), f32, math.log(1e-3), math.log(1e-1)))
    dt_bias = dt + jnp.log(-jnp.expm1(-dt))
    o_norm_w = 1.0 + nrm(ks[12], (DEPTH, DN_HEAD_DIM), 0.02)
    w_out = nrm(ks[13], (DEPTH, D_MODEL, D_MODEL), s_in * DEEPNORM_BETA)
    ln1_g = 1.0 + nrm(ks[14], (DEPTH, D_MODEL), 0.02)
    ln1_b = nrm(ks[15], (DEPTH, D_MODEL), 0.02)
    w_up = nrm(ks[16], (DEPTH, D_MODEL, D_FF_2), s_in)
    w_down = nrm(ks[17], (DEPTH, D_FF_2, D_MODEL), D_FF_2 ** -0.5 * DEEPNORM_BETA)
    ple_gate_w = nrm(ks[18], (DEPTH, D_MODEL, D_MODEL), s_in)
    ple_proj_w = nrm(ks[19], (DEPTH, PLE_DIM, D_MODEL), PLE_DIM ** -0.5 * DEEPNORM_BETA)
    ln2_g = 1.0 + nrm(ks[20], (DEPTH, D_MODEL), 0.02)
    ln2_b = nrm(ks[21], (DEPTH, D_MODEL), 0.02)
    return {"x": x, "p": p, "ln_in_g": ln_in_g, "ln_in_b": ln_in_b, "w_in": w_in,
            "pool_w": pool_w, "pool_scale": pool_scale, "conv_w": conv_w, "a_log": a_log,
            "dt_bias": dt_bias, "o_norm_w": o_norm_w, "w_out": w_out, "ln1_g": ln1_g,
            "ln1_b": ln1_b, "w_up": w_up, "w_down": w_down, "ple_gate_w": ple_gate_w,
            "ple_proj_w": ple_proj_w, "ln2_g": ln2_g, "ln2_b": ln2_b}

def second_block(x, p, ln_in_g, ln_in_b, w_in, pool_w, pool_scale, conv_w, a_log, dt_bias,
              o_norm_w, w_out, ln1_g, ln1_b, w_up, w_down, ple_gate_w, ple_proj_w, ln2_g, ln2_b):
    h = _layer_norm(x, ln_in_g, ln_in_b)
    for i in range(DEPTH):
        proj = h @ w_in[i]
        pool_in, qkv, z, beta_raw, a_raw, gate_a, gate_b = jnp.split(proj, SPLIT_POINTS, axis=-1)
        y_a = _multiscale_pool(pool_in, pool_w[i], pool_scale[i])
        y_b = _gated_deltanet(qkv, z, beta_raw, a_raw, conv_w[i], a_log[i], dt_bias[i], o_norm_w[i])
        mixed = jax.nn.sigmoid(gate_a) * y_a + jax.nn.sigmoid(gate_b) * y_b
        h = _layer_norm(DEEPNORM_ALPHA * h + mixed @ w_out[i], ln1_g[i], ln1_b[i])
        mlp = jnp.square(jax.nn.relu(h @ w_up[i])) @ w_down[i]
        r = DEEPNORM_ALPHA * h + mlp
        ple = jax.nn.sigmoid(r @ ple_gate_w[i]) * (p[i] @ ple_proj_w[i])
        h = _layer_norm(r + ple, ln2_g[i], ln2_b[i])
    return h


_first_inputs_2 = second_inputs


def second_inputs(seed=0):
    import zlib

    import numpy as np

    out = dict(_first_inputs_2(seed))
    spreads = {}
    factors = {'ln_in_g': 2.669,
     'ln_in_b': 2.856,
     'pool_scale': 8.0,
     'a_log': 3.078,
     'o_norm_w': 8.0,
     'ln1_g': 2.812,
     'ln1_b': 2.82,
     'ln2_g': 2.947,
     'ln2_b': 2.748}
    for name, (base, spread) in spreads.items():
        noise = np.random.default_rng([zlib.crc32(name.encode()), seed]).standard_normal(out[name].shape)
        drawn = base * np.exp(spread * noise) if base else spread * noise
        out[name] = __import__('jax').numpy.asarray(drawn.astype(out[name].dtype))
    for name, factor in factors.items():
        out[name] = (out[name] * factor).astype(out[name].dtype)
    return out


_narrow_inputs_2 = second_inputs


def second_inputs(seed=0):

    out = dict(_narrow_inputs_2(seed))
    wider = {'pool_scale': 4.01, 'o_norm_w': 5.76, 'ln2_g': 3.31, 'ln2_b': 3.32}
    for name, times in wider.items():
        mean = out[name].mean()
        out[name] = (mean + times * (out[name] - mean)).astype(out[name].dtype)
    return out


SB_HEADS = 8
SW_HEADS = 8
SW_KV_HEADS = 2
SW_GROUP = SW_HEADS // SW_KV_HEADS
WINDOW_3 = 128
BLOCK = 128
D_FF_3 = 4 * D_MODEL
N_BUCKETS = 32
MAX_DISTANCE = 128

SB_W = SB_HEADS * HEAD_DIM
SW_QW = SW_HEADS * HEAD_DIM
SW_KVW = SW_KV_HEADS * HEAD_DIM
IN_COLS_3 = 3 * SB_W + SW_QW + 2 * SW_KVW + 2 * D_MODEL


def rmsnorm(x, g):
    xf = x.astype(jnp.float32)
    r = lax.rsqrt(jnp.mean(xf * xf, axis=-1, keepdims=True) + EPS)
    return (xf * r).astype(x.dtype) * g

def t5_causal_bucket(dist):
    max_exact = N_BUCKETS // 2
    d = jnp.maximum(dist, 0)
    df = jnp.maximum(d, 1).astype(jnp.float32)
    large = max_exact + (jnp.log(df / max_exact) / math.log(MAX_DISTANCE / max_exact)
                         * (N_BUCKETS - max_exact)).astype(jnp.int32)
    large = jnp.minimum(large, N_BUCKETS - 1)
    return jnp.where(d < max_exact, d, large)

def stick_breaking_attention(q, k, v):
    b_, s_, h_, dh = q.shape
    nb = s_ // BLOCK
    scale = dh ** -0.5
    qb = q.reshape(b_, nb, BLOCK, h_, dh).transpose(1, 0, 3, 2, 4)
    kpos = jnp.arange(s_)

    def one_block(args):
        qblk, n = args
        z = jnp.einsum('bhqd,bshd->bhqs', qblk, k).astype(jnp.float32) * scale
        qpos = n * BLOCK + jnp.arange(BLOCK)
        causal = kpos[None, :] < qpos[:, None]
        log_beta = jax.nn.log_sigmoid(z)
        log_1mb = jnp.where(causal, jax.nn.log_sigmoid(-z), 0.0)
        suffix = lax.cumsum(log_1mb, axis=3, reverse=True) - log_1mb
        a = jnp.where(causal, jnp.exp(log_beta + suffix), 0.0)
        return jnp.einsum('bhqs,bshd->bqhd', a.astype(v.dtype), v)

    o = lax.map(one_block, (qb, jnp.arange(nb)))
    return o.transpose(1, 0, 2, 3, 4).reshape(b_, s_, h_ * dh)

def sliding_window_sink_attention(q, k, v, sinks, bias):
    b_, s_ = q.shape[:2]
    nb = s_ // BLOCK
    scale = HEAD_DIM ** -0.5
    qb = q.reshape(b_, nb, BLOCK, SW_KV_HEADS, SW_GROUP, HEAD_DIM)
    pad = jnp.zeros((b_, BLOCK, SW_KV_HEADS, HEAD_DIM), k.dtype)
    kp = jnp.concatenate([pad, k], axis=1).reshape(b_, nb + 1, BLOCK, SW_KV_HEADS, HEAD_DIM)
    vp = jnp.concatenate([pad, v], axis=1).reshape(b_, nb + 1, BLOCK, SW_KV_HEADS, HEAD_DIM)
    kb = jnp.concatenate([kp[:, :-1], kp[:, 1:]], axis=2)
    vb = jnp.concatenate([vp[:, :-1], vp[:, 1:]], axis=2)
    s = jnp.einsum('bnqkgd,bnskd->bnkgqs', qb, kb).astype(jnp.float32) * scale + bias
    i = jnp.arange(BLOCK)[:, None]
    j = jnp.arange(2 * BLOCK)[None, :]
    dist = BLOCK + i - j
    band = (dist >= 0) & (dist < WINDOW_3)
    key_abs = (jnp.arange(nb)[:, None, None] - 1) * BLOCK + j[None]
    valid = band[None] & (key_abs >= 0)
    s = jnp.where(valid[None, :, None, None], s, -jnp.inf)
    sink = sinks.astype(jnp.float32).reshape(SW_KV_HEADS, SW_GROUP)[None, None, :, :, None, None]
    m = jnp.maximum(jnp.max(s, axis=-1, keepdims=True), sink)
    e = jnp.exp(s - m)
    denom = jnp.sum(e, axis=-1, keepdims=True) + jnp.exp(sink - m)
    pr = (e / denom).astype(v.dtype)
    o = jnp.einsum('bnkgqs,bnskd->bnqkgd', pr, vb)
    return o.reshape(b_, s_, SW_HEADS * HEAD_DIM)

def window_bias(rel_bias):
    i = jnp.arange(BLOCK)[:, None]
    j = jnp.arange(2 * BLOCK)[None, :]
    dist = BLOCK + i - j
    bias = rel_bias[t5_causal_bucket(dist)]
    return bias.transpose(2, 0, 1).reshape(SW_KV_HEADS, SW_GROUP, BLOCK, 2 * BLOCK)

def third_inputs(seed: int = 0) -> dict:
    key = jax.random.key(seed)
    ks = jax.random.split(key, 20)
    f32 = jnp.float32

    def nrm(k, shape, fan_in):
        return jax.random.normal(k, shape, f32) * (fan_in ** -0.5)

    return {
        "x": jax.random.normal(ks[0], (BATCH, SEQ, D_MODEL), f32),
        "p": jax.random.normal(ks[1], (DEPTH, BATCH, SEQ, PLE_DIM), f32),
        "w_in": nrm(ks[2], (DEPTH, D_MODEL, IN_COLS_3), D_MODEL),
        "w_up_a": nrm(ks[3], (DEPTH, SB_W, D_MODEL), SB_W),
        "w_up_b": nrm(ks[4], (DEPTH, SW_QW, D_MODEL), SW_QW),
        "w_o": nrm(ks[5], (DEPTH, D_MODEL, D_MODEL), D_MODEL),
        "w_ff1": nrm(ks[6], (DEPTH, D_MODEL, D_FF_3), D_MODEL),
        "w_ff2": nrm(ks[7], (DEPTH, D_FF_3, D_MODEL), D_FF_3),
        "w_pe": nrm(ks[8], (DEPTH, PLE_DIM, D_MODEL), PLE_DIM),
        "w_pg": nrm(ks[9], (DEPTH, D_MODEL, D_MODEL), D_MODEL),
        "g_mix": 1.0 + 0.01 * jax.random.normal(ks[10], (DEPTH, D_MODEL), f32),
        "g_mlp": 1.0 + 0.01 * jax.random.normal(ks[11], (DEPTH, D_MODEL), f32),
        "g_pe": 1.0 + 0.01 * jax.random.normal(ks[12], (DEPTH, D_MODEL), f32),
        "g_final": 1.0 + 0.01 * jax.random.normal(ks[13], (D_MODEL,), f32),
        "sinks": 0.5 * jax.random.normal(ks[14], (DEPTH, SW_HEADS), f32),
        "rel_bias": 0.5 * jax.random.normal(ks[15], (N_BUCKETS, SW_HEADS), f32),
    }

def third_block(x, p, w_in, w_up_a, w_up_b, w_o, w_ff1, w_ff2, w_pe, w_pg,
              g_mix, g_mlp, g_pe, g_final, sinks, rel_bias):
    b_, s_, _ = x.shape
    bias = window_bias(rel_bias)
    o1 = SB_W
    o2 = o1 + SB_W
    o3 = o2 + SB_W
    o4 = o3 + SW_QW
    o5 = o4 + SW_KVW
    o6 = o5 + SW_KVW
    o7 = o6 + D_MODEL
    for i in range(DEPTH):
        h = rmsnorm(x, g_mix[i])
        proj = h @ w_in[i]
        q_a = proj[..., :o1].reshape(b_, s_, SB_HEADS, HEAD_DIM)
        k_a = proj[..., o1:o2].reshape(b_, s_, SB_HEADS, HEAD_DIM)
        v_a = proj[..., o2:o3].reshape(b_, s_, SB_HEADS, HEAD_DIM)
        q_b = proj[..., o3:o4].reshape(b_, s_, SW_HEADS, HEAD_DIM)
        k_b = proj[..., o4:o5].reshape(b_, s_, SW_KV_HEADS, HEAD_DIM)
        v_b = proj[..., o5:o6].reshape(b_, s_, SW_KV_HEADS, HEAD_DIM)
        gate_a = proj[..., o6:o7]
        gate_b = proj[..., o7:]
        y_a = stick_breaking_attention(q_a, k_a, v_a) @ w_up_a[i]
        y_b = sliding_window_sink_attention(q_b, k_b, v_b, sinks[i], bias) @ w_up_b[i]
        merged = jax.nn.sigmoid(gate_a) * y_a + jax.nn.sigmoid(gate_b) * y_b
        x = x + merged @ w_o[i]
        h = rmsnorm(x, g_mlp[i])
        x = x + jnp.square(jax.nn.relu(h @ w_ff1[i])) @ w_ff2[i]
        pe = p[i] @ w_pe[i]
        x = x + pe * jax.nn.sigmoid(rmsnorm(x, g_pe[i]) @ w_pg[i])
    return rmsnorm(x, g_final)


_first_inputs_3 = third_inputs


def third_inputs(seed=0):
    import zlib

    import numpy as np

    out = dict(_first_inputs_3(seed))
    spreads = {}
    factors = {}
    for name, (base, spread) in spreads.items():
        noise = np.random.default_rng([zlib.crc32(name.encode()), seed]).standard_normal(out[name].shape)
        drawn = base * np.exp(spread * noise) if base else spread * noise
        out[name] = __import__('jax').numpy.asarray(drawn.astype(out[name].dtype))
    for name, factor in factors.items():
        out[name] = (out[name] * factor).astype(out[name].dtype)
    return out


_narrow_inputs_3 = third_inputs


def third_inputs(seed=0):

    out = dict(_narrow_inputs_3(seed))
    wider = {'g_mix': 12.0, 'g_mlp': 7.61, 'g_pe': 12.0, 'g_final': 6.2, 'sinks': 12.0}
    for name, times in wider.items():
        mean = out[name].mean()
        out[name] = (mean + times * (out[name] - mean)).astype(out[name].dtype)
    return out


def setup_inputs(seed=0):
    out = dict(first_inputs(seed))
    for name, value in second_inputs(seed + 1).items():
        if name != "x":
            out[name + "_2"] = value
    for name, value in third_inputs(seed + 2).items():
        if name != "x":
            out[name + "_3"] = value
    return out


def reference(
    x, positions, norm_mix_g, w_in, cmp_k_pos, cmp_k_w1, cmp_k_w2, cmp_v_pos, cmp_v_w1,
    cmp_v_w2, conv_w, conv_b, conv_norm_g, conv_norm_b, w_conv_out, b_conv_out, w_out,
    norm_ffn_g, w_ffn_gate, w_ffn_up, w_ffn_down, norm_final_g, p_2, ln_in_g_2, ln_in_b_2,
    w_in_2, pool_w_2, pool_scale_2, conv_w_2, a_log_2, dt_bias_2, o_norm_w_2, w_out_2, ln1_g_2,
    ln1_b_2, w_up_2, w_down_2, ple_gate_w_2, ple_proj_w_2, ln2_g_2, ln2_b_2, p_3, w_in_3,
    w_up_a_3, w_up_b_3, w_o_3, w_ff1_3, w_ff2_3, w_pe_3, w_pg_3, g_mix_3, g_mlp_3, g_pe_3,
    g_final_3, sinks_3, rel_bias_3,
):
    x = first_block(
        x, positions, norm_mix_g, w_in, cmp_k_pos, cmp_k_w1, cmp_k_w2, cmp_v_pos, cmp_v_w1,
        cmp_v_w2, conv_w, conv_b, conv_norm_g, conv_norm_b, w_conv_out, b_conv_out, w_out,
        norm_ffn_g, w_ffn_gate, w_ffn_up, w_ffn_down, norm_final_g,
    )
    x = second_block(
        x, p_2, ln_in_g_2, ln_in_b_2, w_in_2, pool_w_2, pool_scale_2, conv_w_2, a_log_2,
        dt_bias_2, o_norm_w_2, w_out_2, ln1_g_2, ln1_b_2, w_up_2, w_down_2, ple_gate_w_2,
        ple_proj_w_2, ln2_g_2, ln2_b_2,
    )
    return third_block(
        x, p_3, w_in_3, w_up_a_3, w_up_b_3, w_o_3, w_ff1_3, w_ff2_3, w_pe_3, w_pg_3, g_mix_3,
        g_mlp_3, g_pe_3, g_final_3, sinks_3, rel_bias_3,
    )


_drawn_inputs = setup_inputs


def setup_inputs(seed=0):
    import zlib

    import numpy as np

    out = dict(_drawn_inputs(seed))
    spreads = {}
    factors = {'g_mix_3': 2.69, 'g_pe_3': 19.821, 'sinks_3': 4.763, 'rel_bias_3': 4.497}
    for name, (base, spread) in spreads.items():
        noise = np.random.default_rng([zlib.crc32(name.encode()), seed]).standard_normal(out[name].shape)
        drawn = base * np.exp(spread * noise) if base else spread * noise
        out[name] = __import__('jax').numpy.asarray(drawn.astype(out[name].dtype))
    for name, factor in factors.items():
        out[name] = (out[name] * factor).astype(out[name].dtype)
    return out
```

```python
import math
from contextlib import ExitStack

import numpy as np

import concourse.bass as bass
from concourse import mybir

F32 = mybir.dt.float32
F32R = mybir.dt.float32r
I32 = mybir.dt.int32
ALU = mybir.AluOpType
ACT = mybir.ActivationFunctionType
AX = mybir.AxisListType

P = 128
S = 512
D = 1024
KT = D // P
TT = S // P
NH, DH, NKV = 16, 64, 4
GROUP = NH // NKV
TAPS = 31
NCMP = 31
DFF1 = 2816
NSLICE1 = DFF1 // P
NEG = -1.0e30


PLANS = {
    1: [("conv_gate", 16), ("qk", 16), ("token_major", 5), ("compress", 8), ("attn_gate", 8), ("conv_out", 16), ("attn_out", 8),
        ("ffn_up_0", 16), ("ffn_down_0", 8), ("ffn_up_1", 16), ("ffn_down_1", 8), ("ffn_up_2", 12), ("ffn_down_2", 8)],
    2: [("pool_in", 4), ("qkv", 24), ("beta_a", 1), ("pool_w", 1), ("z_2", 8), ("gate_b_2", 8), ("gate_a_2", 8), ("w_out_2", 8)]
       + [(f"{n}_{q}_2", 8) for q in range(4) for n in ("up", "down")] + [("ple_2", 16)],
    3: [("qk_3", 12), ("kb_3", 1), ("v_3", 5), ("gate_a_3", 8), ("gate_b_3", 8), ("up_3", 8), ("w_o_3", 8)]
       + [(f"{n}_{q}_3", 8) for q in range(4) for n in ("up", "down")] + [("ple_3", 16)],
}


def plan(blocks):
    first, count, n = {}, {}, 0
    for b in blocks:
        for name, k in PLANS[b]:
            first[name], count[name] = n, k
            n += k
    return first, count, n, n + 2 - n % 2


def places(*named):
    at, n = {}, 0
    for name, k in named:
        at[name] = n
        n += k
    return at, n


COLS = {
    1: places(("g_mix", 8), ("conv_w", 8 * TAPS), ("conv_b", 8), ("conv_ng", 8), ("conv_nb", 8), ("b_conv_out", 8),
              ("g_ffn", 8), ("g_final", 8), ("cmp_pos", 32)),
    2: places(("ln_in_g", 8), ("ln_in_b", 8), ("pool_scale", 8), ("conv_w", 96), ("a_log", 8), ("dt_bias", 8), ("o_norm", 1),
              ("ln1_g", 8), ("ln1_b", 8), ("ln2_g", 8), ("ln2_b", 8)),
    3: places(("g_mix", 8), ("g_mlp", 8), ("g_pe", 8), ("g_final", 8), ("sinks", 8)),
}
CONSTS = {
    1: places(("ident", 128), ("ones", 128), ("swap", 128), ("causal", 128), ("cmp_mask", 4 * NCMP), ("cmp_valid", 4),
              ("freq", 1), ("rope_s", 1), ("half_pi", 1)),
    2: places(("ident", 128), ("ones", 128), ("levels", 6 * 128), ("sum64", 128), ("last64", 128), ("mask64", 128),
              ("per_count", 16), ("eps", 1)),
    3: places(("ident", 128), ("ones", 128), ("strict", 128), ("mask_t", 128), ("minus_sum", 128), ("minus_ones", 128), ("turn", 128)),
}
N_COLS = max(n for _, n in COLS.values())
N_CONSTS = max(n for _, n in CONSTS.values())


def constants():
    c = np.zeros((3, P, N_CONSTS), np.float32)

    def put(block, name, a):
        a = np.asarray(a, np.float32).reshape(P, -1)
        at = CONSTS[block][0][name]
        c[block - 1, :, at:at + a.shape[1]] = a

    p = np.arange(P)
    k, m = p[:, None], p[None, :]
    for b in (1, 2, 3):
        put(b, "ident", np.eye(P))
        put(b, "ones", np.ones((P, P)))
    put(1, "swap", ((m % DH < 8) & (k == m + 8)) | ((m % DH >= 8) & (m % DH < 16) & (k == m - 8)))
    put(1, "causal", np.where(m <= k, 0.0, NEG))
    tok = np.arange(S).reshape(TT, P).T
    ends = np.arange(NCMP) * 16 + 31
    put(1, "cmp_mask", np.where(ends[None, None, :] <= tok[:, :, None], 0.0, NEG))
    put(1, "cmp_valid", tok >= 31)
    d = p % DH
    put(1, "freq", np.where(d < 16, np.float32(500000.0) ** (-(d % 8).astype(np.float32) * 2 / 16), 0.0))
    put(1, "rope_s", np.where(d < 8, -1.0, np.where(d < 16, 1.0, 0.0)))
    put(1, "half_pi", np.full(P, np.pi / 2))
    levels = [(m // w % 2 == 1) & (k // w == m // w - 1) for w in (1, 2, 4, 8, 16, 32)]
    put(2, "levels", np.stack(levels, 1))
    put(2, "sum64", (k // 64 == m // 64) & (k <= m))
    put(2, "last64", k == m // 64 * 64 + 63)
    put(2, "mask64", np.where((k // 64 == m // 64) & (k <= m), 0.0, NEG))
    put(2, "per_count", np.broadcast_to(1.0 / np.arange(1, 17), (P, 16)))
    put(2, "eps", np.full(P, 1e-6))
    put(3, "strict", k < m)
    put(3, "mask_t", np.where(k < m, 0.0, NEG))
    put(3, "minus_sum", np.where(k >= m, -1.0, 0.0))
    put(3, "minus_ones", -np.ones((P, P)))
    put(3, "turn", k + m == P - 1)
    return c


def build(nc, t, out, blocks=(1, 2, 3)):
    ctx = ExitStack()
    FIRST, COUNT, LAST, n_units = plan(blocks)
    with ctx:
        def sb(name, shape, dt=F32):
            return ctx.enter_context(nc.sbuf_tensor(name, shape, dt))

        def sem(name):
            return ctx.enter_context(nc.semaphore(name))

        bank = [ctx.enter_context(nc.psum_tensor(f"bank{i}", [P, 512], F32)) for i in range(8)]

        raw = sb("raw", [P, 2, 1024])
        w_hi = sb("w_hi", [P, 2, KT, P], F32R)
        w_lo = sb("w_lo", [P, 2, KT, P], F32R)
        X = sb("X", [P, KT, S])
        act = sb("act", [P, 2, 2, KT, S], F32R)
        BIG = 21744
        big = sb("big", [P, BIG])
        cols = sb("cols", [P, N_COLS])
        cst = sb("cst", [P, N_CONSTS])
        tmp = sb("tmp", [P, 4, S])
        stat = sb("stat", [P, 2, S])
        HI, LO = (act[:, 0, 0], act[:, 1, 0]), (act[:, 0, 1], act[:, 1, 1])
        A, B = 0, 1

        def col(block, name, i=0, n=1):
            return cols[:, bass.ds(COLS[block][0][name] + i, n)]

        def const(block, name, n=1, i=0):
            at = CONSTS[block][0][name] + i
            return cst[:, at:at + n]

        ident, ones = const(1, "ident", 128), const(1, "ones", 128)

        at = [0]

        def region(n):
            a = at[0]
            at[0] += n
            assert at[0] <= BIG, at[0]
            return big[:, a:a + n]

        ZW = S + TAPS - 1
        Z = region(KT * ZW).rearrange("p (c t) -> p c t", t=ZW)
        Z_OUT = Z[:, :, TAPS - 1:]
        QK = region(16 * S).rearrange("p (c t) -> p c t", t=S)
        K_SEL = QK[:, 12:16, :]
        K_WIN = region(NKV * S).rearrange("p (g t) -> p g t", t=S)
        V_TOK = region(5 * TT * P).rearrange("p (u t f) -> p u t f", u=5, t=TT)
        GA = X
        SCR = region(4 * S)
        COS, SIN = SCR[:, 0:S], SCR[:, S:2 * S]
        PT = SCR.rearrange("p (b a t) -> p b a t", b=2, a=2)
        PC = region(TT * NCMP).rearrange("p (q n) -> p q n", q=TT)
        PCT = region(2 * S).rearrange("p (b n) -> p b n", b=2)
        KC_T = region(NKV * NCMP)
        VC_T = region(NKV * DH)
        CW2K = region(2 * P).rearrange("p (c d) -> p c d", c=2)
        CW2V = region(2 * DH).rearrange("p (c d) -> p c d", c=2)
        CST = region(8)
        MX = region(16).rearrange("p (b k) -> p b k", b=2)
        SUMS = region(16).rearrange("p (b k) -> p b k", b=2)
        HID = stat.rearrange("p a t -> p (a t)")[:, 0:4 * 124].rearrange("p (m c n) -> p m c n", m=2, c=2)

        at[0] = 0
        PAD = 3
        QKV = region(24 * (S + PAD)).rearrange("p (c t) -> p c t", t=S + PAD)
        QKV_T = QKV[:, :, PAD:]
        OUT2 = QKV_T[:, 16:24]
        YA = QKV_T[:, 0:8]
        HT = region(12 * TT * 8).rearrange("p (x q h) -> p x q h", x=12, q=TT)
        BETA, DEC, GC, EGC, EGLC, BE, SPS, SPA, SPU, SPL, SPW, EXA = (HT[:, i] for i in range(12))
        ROWS = region(2 * S).rearrange("p (x t) -> p x t", x=2)
        after_heads = at[0]
        U_POOL = region(4 * (S + 16)).rearrange("p (c t) -> p c t", t=S + 16)
        WIN = region(2 * (S + 16)).rearrange("p (c t) -> p c t", t=S + 16)
        BA = region(TT * 16).rearrange("p (q c) -> p q c", q=TT)
        at[0] = after_heads
        tile4 = lambda: region(S).rearrange("p (q n) -> p q n", q=TT)
        DT, MT, TM, VB, KBE = (tile4() for _ in range(5))
        UM = DT
        XM, CT = (x.rearrange("p (q n) -> p q n", q=TT) for x in (stat[:, 0], tmp[:, 2]))
        KBT = tmp[:, 3].rearrange("p (q n) -> p q n", q=TT)
        ATT, KG, UV = ([tile4(), tile4()] for _ in range(3))
        WT, QG = ([region(S), region(S)] for _ in range(2))
        VNEW, ST = region(P), region(P)
        EGL = region(16).rearrange("p (b c) -> p b c", b=2)

        at[0] = 0
        QKB = region(13 * S).rearrange("p (c t) -> p c t", t=S)
        KBD = region(2 * S).rearrange("p (g t) -> p g t", t=S)
        V3 = region(5 * TT * P).rearrange("p (u t f) -> p u t f", u=5, t=TT)
        GATE_A, GATE_B = (big[:, a:a + KT * S].rearrange("p (c t) -> p c t", t=S) for a in (0, KT * S))
        BIAS = region(8 * 256).rearrange("p (h n) -> p h n", h=8)
        LS = region(8 * S).rearrange("p (b a t) -> p b a t", b=2, a=TT)
        BIAS_T = LS[:, 1].rearrange("p a t -> p (a t)").rearrange("p (h n) -> p h n", h=8)
        P3 = LS[:, 0, 0:2, :]
        SC = region(TT * 256).rearrange("p (n k) -> p n k", n=TT)
        PB = region(TT * 256).rearrange("p (n k) -> p n k", n=TT)
        PTB = region(TT * 256).rearrange("p (n k) -> p n k", n=TT)
        SW = region(24).rearrange("p (x n) -> p x n", x=6)
        REL, HOT, BROW = SC[:, 0, 0:8], PB.rearrange("p n k -> p (n k)")[:, 0:384], PTB.rearrange("p n k -> p (n k)")[:, 0:384]
        bias_rows = nc.dram_tensor("bias_rows", (8, 384), F32, kind="Internal").ap() if 3 in blocks else None

        params_in = sem("params_in")
        x_in = sem("x_in")
        w_loaded = [sem("w_loaded_even"), sem("w_loaded_odd")]
        w_hi_ready, w_lo_ready = sem("w_hi_ready"), sem("w_lo_ready")
        mm_done = sem("mm_done")
        act_read, dve_read = sem("act_read"), sem("dve_read")
        sq_ready, sq_summed, mean_ready = sem("sq_ready"), sem("sq_summed"), sem("mean_ready")
        var_ready, rstd_ready, centered = sem("var_ready"), sem("rstd_ready"), sem("centered")
        full_made, hi_made, lo_made = sem("full_made"), sem("hi_made"), sem("lo_made")
        dve_step, act_step = sem("dve_step"), sem("act_step")
        pad_cleared, conv_tap, conv_done = sem("pad_cleared"), sem("conv_tap"), sem("conv_done")
        rope_table, swapped, roped = sem("rope_table"), sem("swapped"), sem("roped")
        pair_keys_in, keys_in, x_back, out_stored = sem("pair_keys_in"), sem("keys_in"), sem("x_back"), sem("out_stored")
        blocks_made, hidden_sum, hidden_ready, cmp_sum, cmp_ready = (
            sem("blocks_made"), sem("hidden_sum"), sem("hidden_ready"), sem("cmp_sum"), sem("cmp_ready"))
        qk_done, neg_ready, exp_done, scaled, tr_done, pt_act, pt_dve, pv_done, merged = (
            sem(n) for n in ("qk_done", "neg_ready", "exp_done", "scaled", "tr_done", "pt_act", "pt_dve", "pv_done", "merged"))

        c_scores, c_shifted, c_exp, c_scaled, c_tr, c_kept = (
            sem(n) for n in ("c_scores", "c_shifted", "c_exp", "c_scaled", "c_tr", "c_kept"))
        z_ready, sp_ready, l_ready, suffixed, a_ready, pv3_done, y_kept = (
            sem(n) for n in ("z_ready", "sp_ready", "l_ready", "suffixed", "a_ready", "pv3_done", "y_kept"))
        sw_qk, sw_kept, sw_neg, sw_exp, sw_scaled, sw_tr, sw_pt_act, sw_pt_dve, sw_pv = (
            sem(n) for n in ("sw_qk", "sw_kept", "sw_neg", "sw_exp", "sw_scaled", "sw_tr", "sw_pt_act", "sw_pt_dve", "sw_pv"))
        rel_in, rel_fill, bias_sum, bias_kept, bias_out, bias_in, kb_in, q_scaled, bias_turned, bias_placed = (
            sem(n) for n in ("rel_in", "rel_fill", "bias_sum", "bias_kept", "bias_out", "bias_in", "kb_in", "q_scaled",
                             "bias_turned", "bias_placed"))
        pooled_mm, z_gate, gated_2, relu_made, p_in, x_added = (
            sem(n) for n in ("pooled_mm", "z_gate", "gated_2", "relu_made", "p_in", "x_added"))
        rope_sin, o_read, normed = sem("rope_sin"), sem("o_read"), sem("normed")

        chunk_ready = sem("chunk_ready")
        window_step, pooled, conv4_tap, conv4_done, silu_done, pool_scaled = (
            sem(n) for n in ("window_step", "pooled", "conv4_tap", "conv4_done", "silu_done", "pool_scaled"))
        l2_sq, l2_sum, l2_rstd, l2_done = (sem(n) for n in ("l2_sq", "l2_sum", "l2_rstd", "l2_done"))
        sp_in, sp_log, dec_ready, gc_sum, gc_kept, rows_tr, rows_kept, decays = (
            sem(n) for n in ("sp_in", "sp_log", "dec_ready", "gc_sum", "gc_kept", "rows_tr", "rows_kept", "decays"))
        rows_done, tok_done, kk_done, t_done, x_done, y_done, uw_done = (
            sem(n) for n in ("rows_done", "tok_done", "kk_done", "t_done", "x_done", "y_done", "uw_done"))
        eg_done, arg_done, dt_done, kb_done, tokv_done, m_done, ct_ready, u_ready, t_ready, x_kept, uv_ready, wt_ready = (
            sem(n) for n in ("eg_done", "arg_done", "dt_done", "kb_done", "tokv_done", "m_done", "ct_ready", "u_ready",
                             "t_ready", "x_kept", "uv_ready", "wt_ready"))
        vn_done, vnew_ready, ds_done, s_ready, o_done, o_sq, o_sum, o_rstd, o_kept = (
            sem(n) for n in ("vn_done", "vnew_ready", "ds_done", "s_ready", "o_done", "o_sq", "o_sum", "o_rstd", "o_kept"))

        class Count(dict):

            def __missing__(self, k):
                return 0

            def add(self, k, n=1):
                self[k] = self[k] + n
                return self[k]

        block = ctx.enter_context(nc.Block())

        @block.sync
        def _(sp):
            for u in range(2):
                sp.dma_start(raw[:, u], t["w"][u]).then_inc(w_loaded[u], 16)
            with sp.Fori(1, n_units // 2) as i:
                for u in range(2):
                    sp.wait_ge(w_hi_ready, 2 * i + u - 1)
                    sp.wait_ge(w_lo_ready, 2 * i + u - 1)
                    sp.dma_start(raw[:, u], t["w"][2 * i + u]).then_inc(w_loaded[u], 16)

        @block.gpsimd
        def _(pool):
            if 1 in blocks:
                pool.memset(Z[:, :, 0:TAPS - 1], 0.0).then_inc(pad_cleared, 1)
            with pool.Fori(0, n_units // 2) as i:
                for u in range(2):
                    pool.wait_ge(w_hi_ready, 2 * i + u + 1)
                    pool.tensor_tensor(w_lo[:, u], raw[:, u].rearrange("p (k n) -> p k n", k=KT),
                                       w_hi[:, u].bitcast(F32), ALU.subtract).then_inc(w_lo_ready, 1)

        @block.scalar
        def _(a):
            c = Count()

            def link(ins):
                ins.then_inc(act_step, 1)
                a.wait_ge(act_step, c.add("step"))

            def load_params(b):
                a.dma_start(cols[:], t["cols"][b - 1]).then_inc(params_in, 16)
                a.dma_start(cst[:], t["consts"][b - 1]).then_inc(params_in, 16)

            def split_hi(U, u):
                a.wait_ge(w_loaded[u], (U - u) * 8 + 16)
                a.wait_ge(mm_done, U - 1)
                a.copy(w_hi[:, u].rearrange("p k n -> p (k n)"), raw[:, u]).then_inc(w_hi_ready, 1)

            def split_rest(done):
                for U in range(done, n_units):
                    split_hi(U, U % 2)

            def tables(name):
                a.preload_act_table_set(name)

            LOG_EXP, SIGMOID, SILU = "natural_log_exp_and_others", "sigmoid_and_others", "silu_and_others"

            def rstd():
                a.wait_ge(var_ready, c.add("var"))
                link(a.activation(stat[:, 0], stat[:, 0], ACT.Ln))
                a.activation(stat[:, 1], stat[:, 0], ACT.Exp, scale=-0.5).then_inc(rstd_ready, 1)

            def squares(src, ready=None):
                tables(LOG_EXP)
                for k in range(KT):
                    if ready:
                        ready(k)
                    if c["sq"] >= 2:
                        a.wait_ge(sq_summed, c["sq"] - 1)
                    a.activation(tmp[:, k % 2], src[:, k], ACT.Square).then_inc(sq_ready, 1)
                    c.add("sq")

            def loop(name, epilogue=None):
                first, n = FIRST[name], COUNT[name]
                with a.Fori(0, n // 2) as i:
                    for u in range(2):
                        s = (first + u) % 2
                        split_hi(first + 2 * i + u + 1, 1 - s)
                        if epilogue:
                            epilogue(i, u, first + 2 * i + u, s)

            def gate(func):
                base, used = c["read"], c["dve_read"]

                def epilogue(i, u, U, s):
                    if u == 0:
                        a.wait_ge(mm_done, U + 1)
                        a.wait_ge(dve_read, used + i)
                        a.activation(tmp[:, 2], bank[s][:], func).then_inc(act_read, 1)
                return epilogue

            def gated(name, func):
                tables(SIGMOID if func == ACT.Sigmoid else SILU)
                loop(name, gate(func))
                c.add("read", COUNT[name] // 2)
                c.add("dve_read", COUNT[name] // 2)

            def block_1():
                a.dma_start(CW2K, t["cw2k"]).then_inc(params_in, 16)
                a.dma_start(CW2V, t["cw2v"]).then_inc(params_in, 16)
                a.dma_start(tmp[:, 3].bitcast(I32), t["pos"]).then_inc(params_in, 16)
                squares(X)
                rstd()
                a.wait_ge(rope_table, 1)
                link(a.activation(COS, SIN, ACT.Abs))
                a.activation(SIN, SIN, ACT.Sin).then_inc(rope_table, 1)
                a.activation(COS, COS, ACT.Sin, bias=const(1, "half_pi"), scale=-1.0).then_inc(rope_table, 1)

                gated("conv_gate", ACT.Sigmoid)
                def keep_qk(i, u, U, s):
                    a.wait_ge(mm_done, U + 1)
                    a.copy(QK[:, bass.ds(2 * i + u, 1), :].rearrange("p a t -> p (a t)"), bank[s][:]).then_inc(act_read, 1)
                loop("qk", keep_qk)
                c.add("read", 16)

                for k in range(5):
                    U = FIRST["token_major"] + k
                    split_hi(U + 1, (U + 1) % 2)
                    a.wait_ge(mm_done, U + 1)
                    a.activation(V_TOK[:, k].rearrange("p t f -> p (t f)"), bank[U % 2][:],
                                 ACT.Sigmoid if k == 4 else ACT.Copy).then_inc(act_read, 1)
                c.add("read", 5)

                a.wait_ge(roped, 14)
                for m in range(2):
                    for g in range(NKV):
                        src = QK[(g % 2) * DH:(g % 2) * DH + DH, 12 + 2 * m + g // 2, :]
                        a.dma_start(X[0:DH, 4 * m + g, :], src).then_inc(pair_keys_in, 16)
                        a.dma_start(X[DH:P, 4 * m + g, 0:S - 1], src[:, 1:S]).then_inc(pair_keys_in, 16)
                for g in range(NKV):
                    for h in range(2):
                        a.dma_start(K_WIN[h * DH:h * DH + DH, g, :],
                                    QK[(g % 2) * DH:(g % 2) * DH + DH, 10 + g // 2, :]).then_inc(keys_in, 16)
                a.wait_ge(pair_keys_in, 16 * 16)
                for g in range(NKV):
                    for h in range(2):
                        a.dma_start(K_SEL[h * DH:h * DH + DH, g, :],
                                    QK[(g % 2) * DH:(g % 2) * DH + DH, 8 + g // 2, :]).then_inc(keys_in, 16)

                for k in range(8):
                    U = FIRST["compress"] + k
                    split_hi(U + 1, (U + 1) % 2)
                    if k % 2:
                        m, mt = k // 4, k // 2 % 2
                        a.wait_ge(mm_done, U + 1)
                        a.activation(HID[:, m, mt], bank[2 + k // 2][:, 0:124], ACT.Silu).then_inc(hidden_ready, 1)
                a.wait_ge(cmp_sum, 1)
                a.copy(KC_T, bank[6][:, 0:124]).then_inc(cmp_ready, 1)
                a.wait_ge(cmp_sum, 2)
                a.copy(VC_T[0:NCMP, :], bank[7][0:NCMP, 0:NKV * DH]).then_inc(cmp_ready, 1)

                def keep_gate(i, u, U, s):
                    a.wait_ge(mm_done, U + 1)
                    a.activation(GA[:, bass.ds(2 * i + u, 1), :].rearrange("p a t -> p (a t)"), bank[s][:],
                                 ACT.Sigmoid).then_inc(act_read, 1)
                a.wait_ge(blocks_made, 2)
                tables(SIGMOID)
                loop("attn_gate", keep_gate)
                c.add("read", 8)
                a.wait_ge(lo_made, KT)
                base = c["centered"]
                squares(Z_OUT, lambda k: a.wait_ge(centered, base + k + 1))
                c.add("centered", KT)
                rstd()
                for k in range(KT):
                    if k == 0:
                        tables(SILU)
                    a.wait_ge(centered, c.add("centered"))
                    if k >= 2:
                        a.wait_ge(lo_made, KT + k - 1)
                    a.activation(tmp[:, k % 2], Z_OUT[:, k], ACT.Silu, bias=col(1, "conv_nb", k),
                                 scale=col(1, "conv_ng", k)).then_inc(full_made, 1)
                gated("conv_out", ACT.Sigmoid)

                def exps(n):
                    h, qt, b = n // 4, n % 4, n % 2
                    kw = (qt + 1) * P
                    a.wait_ge(neg_ready, n + 1)
                    if n >= 2:
                        a.wait_ge(tr_done, n - 1)
                        a.wait_ge(scaled, 2 * n - 2)
                    for j in range(2):
                        a.activation(tmp[:, 2 * b + j, 0:kw], bank[2 + 2 * b + j][:, 0:kw], ACT.Exp, bias=MX[:, b, 2 + j:3 + j],
                                     scale=0.125, accum_out=SUMS[:, b, j:j + 1]).then_inc(exp_done, 1)

                def keep_pt(n):
                    a.wait_ge(tr_done, n + 1)
                    if n >= 2:
                        a.wait_ge(pv_done, n - 1)
                    kw = (n % 4 + 1) * P
                    a.copy(PT[:, n % 2, 0, 0:kw], bank[0][:, 0:kw]).then_inc(pt_act, 1)

                def compressed_exp(h):
                    a.wait_ge(c_shifted, h + 1)
                    a.activation(PC, PC, ACT.Exp, scale=0.125).then_inc(c_exp, 1)

                a.wait_ge(dve_read, c["dve_read"])
                compressed_exp(0)
                for n in range(NH * TT + 1):
                    if n < NH * TT:
                        exps(n)
                    if n % 4 == 1 and n // 4 + 1 < NH:
                        compressed_exp(n // 4 + 1)
                    if n >= 1:
                        keep_pt(n - 1)
                    if n >= 1 and n % 8 == 1 and n > 8:
                        hp = n // 8 - 1
                        a.wait_ge(merged, hp + 1)
                        a.dma_start(X[:, hp], t["x"][:, hp]).then_inc(x_back, 16)
                a.wait_ge(merged, 8)
                a.dma_start(X[:, 7], t["x"][:, 7]).then_inc(x_back, 16)
                loop("attn_out")

                def residual_norm():
                    base = c["dve_read"]
                    squares(X, lambda k: a.wait_ge(dve_read, base + k + 1))
                    c.add("dve_read", KT)
                    rstd()
                a.wait_ge(x_back, 128)
                residual_norm()
                for q in range(3):
                    gated(f"ffn_up_{q}", ACT.Silu)
                    loop(f"ffn_down_{q}")
                    if q < 2:
                        c.add("dve_read", 8)
                residual_norm()
                c.add("normed", KT)

            def layer_norm():
                base = c["centered"]
                squares(X, lambda k: a.wait_ge(centered, base + k + 1))
                c.add("centered", KT)
                rstd()

            def block_2():
                layer_norm()

                def keep(dst):
                    def epilogue(i, u, U, s):
                        a.wait_ge(mm_done, U + 1)
                        a.copy(dst[:, bass.ds(2 * i + u, 1), :].rearrange("p a t -> p (a t)"), bank[s][:]).then_inc(act_read, 1)
                    return epilogue
                loop("pool_in", keep(U_POOL[:, :, 16:]))
                loop("qkv", keep(QKV_T))
                U = FIRST["beta_a"]
                split_hi(U + 1, (U + 1) % 2)
                a.wait_ge(mm_done, U + 1)
                a.copy(BA, bank[U % 2].rearrange("p (q n) -> p q n", q=TT)[:, :, 0:16]).then_inc(act_read, 1)
                c.add("read", 4 + 24 + 1)
                a.wait_ge(act_read, c["read"])
                link(a.activation(BETA, BA[:, :, 0:8], ACT.Sigmoid))
                for k in range(24):
                    a.wait_ge(conv4_done, k + 1)
                    a.activation(QKV_T[:, k], QKV_T[:, k], ACT.Silu).then_inc(silu_done, 1)
                a.wait_ge(silu_done, 24)
                tables(LOG_EXP)

                def l2_square(k):
                    if k >= 2:
                        a.wait_ge(l2_sum, k - 1)
                    a.activation(tmp[:, k % 2], QKV_T[:, k], ACT.Square).then_inc(l2_sq, 1)
                a.wait_ge(sp_in, 1)
                link(a.activation(SPA, SPS, ACT.Abs))
                link(a.activation(SPU, SPA, ACT.Exp, scale=-1.0))
                link(a.activation(EXA[:, 0], col(2, "a_log", 0, 8), ACT.Exp))
                a.activation(SPL, SPU, ACT.Ln, bias=1.0).then_inc(sp_log, 1)
                l2_square(0)
                for k in range(16):
                    if k + 1 < 16:
                        l2_square(k + 1)
                    a.wait_ge(l2_sum, k + 1)
                    if k >= 2:
                        a.wait_ge(l2_done, k - 1)
                    link(a.activation(tmp[:, 2 + k % 2], bank[6 + k % 2][:], ACT.Ln, bias=const(2, "eps")))
                    a.activation(tmp[:, 2 + k % 2], tmp[:, 2 + k % 2], ACT.Exp, scale=-0.5).then_inc(l2_rstd, 1)
                a.wait_ge(gc_kept, 2)
                link(a.activation(EGC, GC, ACT.Exp))
                a.activation(EGLC, EGLC, ACT.Exp).then_inc(decays, 1)

                EG = stat[:, 1]

                def prepare(h, slot):
                    if slot == 0:
                        a.wait_ge(rows_done, h + 1)
                        if h:
                            a.wait_ge(kb_done, h)
                        a.activation(EG, bank[2][:], ACT.Exp).then_inc(eg_done, 1)
                        a.wait_ge(arg_done, h + 1)
                        a.activation(DT.rearrange("p q n -> p (q n)"), DT.rearrange("p q n -> p (q n)"), ACT.Exp).then_inc(dt_done, 1)
                    if 3 <= slot < 8:
                        a.wait_ge(x_done, 5 * h + slot - 2)
                        a.copy(XM.rearrange("p q n -> p (q n)"), bank[5][:]).then_inc(x_kept, 1)
                    if slot == 8:
                        a.wait_ge(uw_done, h + 1)
                        if h >= 2:
                            a.wait_ge(vnew_ready, 8 * h - 8)
                        a.copy(UV[h % 2].rearrange("p q n -> p (q n)"), bank[4][:]).then_inc(uv_ready, 1)

                def o_factor(h):
                    a.wait_ge(o_done, h + 1)
                    a.activation(tmp[:, 0], bank[0][:], ACT.Square).then_inc(o_sq, 1)
                    a.wait_ge(o_sum, h + 1)
                    if h:
                        a.wait_ge(o_kept, h)
                    link(a.activation(tmp[:, 1], bank[1][:], ACT.Ln, scale=1.0 / P, bias=const(2, "eps")))
                    a.activation(tmp[:, 1], tmp[:, 1], ACT.Exp, scale=-0.5).then_inc(o_rstd, 1)

                a.wait_ge(l2_done, 16)
                tables(LOG_EXP)
                for h in range(9):
                    for slot in range(9):
                        if h < 8:
                            prepare(h, slot)
                        if h >= 1 and slot == 8:
                            o_factor(h - 1)

                U = FIRST["pool_w"]
                split_hi(U + 1, (U + 1) % 2)
                for j in range(KT):
                    a.wait_ge(pooled_mm, j + 1) if j < KT - 1 else a.wait_ge(mm_done, U + 1)
                    a.activation(YA[:, j], bank[2 + j % 2][:], ACT.Copy, scale=col(2, "pool_scale", j)).then_inc(pool_scaled, 1)

                def gate_into_tmp(name, func, reader_count):
                    g = c["gated"]

                    def epilogue(i, u, U, s):
                        a.wait_ge(mm_done, U + 1)
                        a.wait_ge(gated_2, g + 2 * i + u)
                        a.activation(tmp[:, 2 + u], bank[s][:], func).then_inc(reader_count, 1)
                    loop(name, epilogue)
                    c.add("gated", 8)
                a.wait_ge(o_kept, 8)
                a.wait_ge(l2_done, 16)
                tables(SIGMOID)
                gate_into_tmp("z_2", ACT.Sigmoid, z_gate)
                gate_into_tmp("gate_b_2", ACT.Sigmoid, act_read)
                gate_into_tmp("gate_a_2", ACT.Sigmoid, act_read)
                c.add("read", 16)
                c.add("dve_read", 8)
                loop("w_out_2")
                c.add("dve_read", 8)
                layer_norm()
                for q in range(4):
                    loop(f"up_{q}_2")
                    loop(f"down_{q}_2")
                c.add("dve_read", 64)
                a.wait_ge(sq_summed, c["sq"])
                a.dma_start(tmp[:, 0:2], t["p2"]).then_inc(p_in, 16)
                gated("ple_2", ACT.Sigmoid)
                a.wait_ge(x_added, 8)
                layer_norm()
                c.add("normed", KT)

            def block_3():
                a.wait_ge(rel_fill, 1)
                a.dma_start(REL[0:32], t["rel"]).then_inc(rel_in, 16)
                a.dma_start(HOT[0:33], t["bucket"]).then_inc(rel_in, 16)
                squares(X)
                rstd()
                a.wait_ge(bias_sum, 1)
                a.copy(BROW[0:8], bank[5][0:8, 0:384]).then_inc(bias_kept, 1)
                a.wait_ge(bias_kept, 1)
                a.dma_start(bias_rows, BROW[0:8]).then_inc(bias_out, 16)
                a.wait_ge(bias_out, 16)
                a.dma_start(BIAS_T, bass.AP(tensor=bias_rows.tensor, offset=0, ap=[[1, P], [384, 8], [1, 256]])).then_inc(bias_in, 16)

                def keep(i, u, U, s):
                    a.wait_ge(mm_done, U + 1)
                    a.copy(QKB[:, bass.ds(2 * i + u, 1), :].rearrange("p a t -> p (a t)"), bank[s][:]).then_inc(act_read, 1)
                loop("qk_3", keep)
                for k in range(4):
                    a.wait_ge(bias_turned, k + 1)
                    a.copy(BIAS[:, 2 * k:2 * k + 2].rearrange("p h n -> p (h n)"), bank[2 + k][:]).then_inc(bias_placed, 1)
                for k in range(6):
                    U = FIRST["kb_3"] + k
                    split_hi(U + 1, (U + 1) % 2)
                    a.wait_ge(mm_done, U + 1)
                    a.copy(QKB[:, 12] if k == 0 else V3[:, k - 1].rearrange("p t f -> p (t f)"), bank[U % 2][:]).then_inc(act_read, 1)
                c.add("read", 18)
                a.wait_ge(act_read, c["read"])
                for g in range(2):
                    for h in range(2):
                        a.dma_start(KBD[h * DH:h * DH + DH, g, :], QKB[g * DH:g * DH + DH, 12, :]).then_inc(kb_in, 16)

                def softplus_tail(m):
                    w = S - P * (3 - m % 4)
                    a.wait_ge(z_ready, m + 1)
                    if m >= 2:
                        a.wait_ge(l_ready, m - 1)
                    e = stat[:, m % 2, 0:w]
                    link(a.activation(e, bank[2 + m % 4][:, 0:w], ACT.Abs))
                    link(a.activation(e, e, ACT.Exp, scale=-1.0))
                    a.activation(e, e, ACT.Ln, bias=1.0).then_inc(sp_ready, 1)

                def weights(m):
                    w = S - P * (3 - m % 4)
                    a.wait_ge(suffixed, m + 1)
                    if m >= 4:
                        a.wait_ge(pv3_done, m - 3)
                    a.activation(tmp[:, m % 4, 0:w], bank[2 + m % 4][:, 0:w], ACT.Exp).then_inc(a_ready, 1)

                tables(LOG_EXP)
                for m in range(33):
                    if m < 32:
                        softplus_tail(m)
                    if m >= 1:
                        weights(m - 1)

                def window_exps(h):
                    a.wait_ge(sw_neg, h + 1)
                    if h:
                        a.wait_ge(sw_tr, h)
                        a.wait_ge(sw_scaled, h)
                    a.activation(SW[:, 4], SW[:, 2], ACT.Exp)
                    for n in range(TT):
                        lo = P if n == 0 else 0
                        ins = a.activation(PB[:, n, lo:], SC[:, n, lo:], ACT.Exp, bias=SW[:, 1, n:n + 1], accum_out=SW[:, 3, n:n + 1])
                    ins.then_inc(sw_exp, 1)

                def window_pt(h):
                    a.wait_ge(sw_tr, h + 1)
                    if h:
                        a.wait_ge(sw_pv, h)
                    a.copy(PTB.rearrange("p n k -> p (n k)")[:, P:512], bank[4][:, P:512]).then_inc(sw_pt_act, 1)

                for h in range(9):
                    if h < 8:
                        window_exps(h)
                    if h >= 1:
                        window_pt(h - 1)

                def keep_gates(dst):
                    def epilogue(i, u, U, s):
                        a.wait_ge(mm_done, U + 1)
                        a.activation(dst[:, bass.ds(2 * i + u, 1), :].rearrange("p a t -> p (a t)"), bank[s][:],
                                     ACT.Sigmoid).then_inc(act_read, 1)
                    return epilogue
                a.wait_ge(sw_pv, 8)
                a.dma_start(P3, t["p3"]).then_inc(p_in, 16)
                tables(SIGMOID)
                loop("gate_a_3", keep_gates(GATE_A))
                loop("gate_b_3", keep_gates(GATE_B))
                c.add("read", 16)
                loop("up_3")
                c.add("dve_read", 8)

                def residual_norm(name):
                    base = c[name]
                    squares(X, lambda k: a.wait_ge(x_added if name == "added" else dve_read, base + k + 1))
                    c.add(name, KT)
                    rstd()
                loop("w_o_3")
                residual_norm("dve_read")
                for q in range(4):
                    loop(f"up_{q}_3")
                    loop(f"down_{q}_3")
                c.add("dve_read", 56)
                residual_norm("dve_read")
                gated("ple_3", ACT.Sigmoid)
                c["added"] = 8 if 2 in blocks else 0
                residual_norm("added")
                c.add("normed", KT)

            a.dma_start(X[:], t["x"]).then_inc(x_in, 16)
            load_params(blocks[0])
            a.wait_ge(w_loaded[0], 16)
            a.copy(w_hi[:, 0].rearrange("p k n -> p (k n)"), raw[:, 0]).then_inc(w_hi_ready, 1)
            a.wait_ge(x_in, 16)
            for b in blocks:
                if b != blocks[0]:
                    a.wait_ge(normed, c["normed"])
                    load_params(b)
                {1: block_1, 2: block_2, 3: block_3}[b]()
            split_rest(LAST + 1)
            a.wait_ge(normed, c["normed"])
            a.dma_start(out, X[:]).then_inc(out_stored, 16)
            a.wait_ge(out_stored, 16)

        @block.vector
        def _(v):
            c = Count()

            def link(ins):
                ins.then_inc(dve_step, 1)
                v.wait_ge(dve_step, c.add("step"))

            def variance(eps=1e-6):
                v.wait_ge(sq_summed, c.add("sq", KT))
                v.tensor_scalar(stat[:, 0], bank[7][:], 1.0 / D, eps, ALU.mult, ALU.add).then_inc(var_ready, 1)
                v.wait_ge(rstd_ready, c.add("rstd"))

            def split(n, make, dst):
                full, made = c["full"], c["made"]
                for k in range(n + 1):
                    if k < n:
                        if k >= 2:
                            v.wait_ge(lo_made, made + k - 1)
                        make(k, tmp[:, k % 2])
                    if k >= 1:
                        j = k - 1
                        v.wait_ge(full_made, full + j + 1)
                        v.tensor_copy(HI[dst][:, j], tmp[:, j % 2]).then_inc(hi_made, 1)
                        v.wait_ge(hi_made, made + j + 1)
                        v.tensor_tensor(LO[dst][:, j], tmp[:, j % 2], HI[dst][:, j].bitcast(F32), ALU.subtract)\
                         .then_inc(lo_made, 1)
                c.add("full", n)
                c.add("made", n)

            def rms_norm(gain, dst, block=1):
                variance()
                split(KT, lambda k, to: v.scalar_tensor_tensor(
                    to, X[:, k], col(block, gain, k), stat[:, 1], ALU.mult, ALU.mult).then_inc(full_made, 1), dst)

            def residual_add(name, factor=None):
                first = FIRST[name]
                with v.Fori(0, COUNT[name] // 2) as i:
                    for u in range(2):
                        x = X[:, bass.ds(2 * i + u, 1), :].rearrange("p a t -> p (a t)")
                        v.wait_ge(mm_done, first + 2 * i + u + 1)
                        o = bank[(first + u) % 2][:]
                        (v.tensor_tensor(x, x, o, ALU.add) if factor is None else
                         v.scalar_tensor_tensor(x, x, factor, o, ALU.mult, ALU.add)).then_inc(dve_read, 1)
                c.add("dve_read", 8)

            def gated_operands(name, dst):
                first, n = FIRST[name], COUNT[name] // 2
                reads, used, made = c["act_read"], c["dve_read"], c["made"]
                v.wait_ge(mm_done, first)
                with v.Fori(0, n) as i:
                    v.wait_ge(act_read, reads + i + 1)
                    v.wait_ge(mm_done, first + 2 * i + 2)
                    v.wait_ge(lo_made, made + i)
                    v.tensor_tensor(tmp[:, 3], bank[(first + 1) % 2][:], tmp[:, 2], ALU.mult).then_inc(dve_read, 1)
                    v.wait_ge(dve_read, used + i + 1)
                    hi = HI[dst][:, bass.ds(i, 1), :].rearrange("p a t -> p (a t)")
                    lo = LO[dst][:, bass.ds(i, 1), :].rearrange("p a t -> p (a t)")
                    v.tensor_copy(hi, tmp[:, 3]).then_inc(hi_made, 1)
                    v.wait_ge(hi_made, made + i + 1)
                    v.tensor_tensor(lo, tmp[:, 3], hi.bitcast(F32), ALU.subtract).then_inc(lo_made, 1)
                c.add("act_read", n)
                c.add("dve_read", n)
                c.add("made", n)

            def block_1():
                v.wait_ge(params_in, c.add("params", 16 * 5))
                ang, turns = tmp[:, 2], SIN
                link(v.tensor_copy(ang, tmp[:, 3].bitcast(I32)))
                link(v.tensor_scalar(ang, ang, const(1, "freq"), None, ALU.mult))
                link(v.tensor_scalar(turns, ang, 1.0 / (2 * np.pi), None, ALU.mult))
                link(v.tensor_scalar(turns, turns, 12582912.0, None, ALU.add))
                link(v.tensor_scalar(turns, turns, -12582912.0, None, ALU.add))
                parts = [6.28125, 0.0019340515136718750]
                parts.append(2 * np.pi - sum(parts))
                for part in parts:
                    link(v.scalar_tensor_tensor(ang, turns, -part, ang, ALU.mult, ALU.add))
                v.tensor_scalar(SIN, ang, 3.1415925, -3.1415925, ALU.min, ALU.max).then_inc(rope_table, 1)

                rms_norm("g_mix", A)

                def conv_gate(i):
                    g = 2 * i + 1
                    v.wait_ge(act_read, i + 1)
                    v.wait_ge(mm_done, FIRST["conv_gate"] + g + 1)
                    v.tensor_tensor(Z[:, bass.ds(i, 1), TAPS - 1:].rearrange("p a t -> p (a t)"),
                                    bank[1][:], tmp[:, 2], ALU.mult).then_inc(dve_read, 1)
                with v.Fori(0, 8) as i:
                    conv_gate(i)
                c.add("dve_read", 8)
                v.wait_ge(pad_cleared, 1)
                v.wait_ge(dve_read, 8)

                with v.Fori(0, 4) as i:
                    v.wait_ge(conv_done, 2 * i)
                    for j in range(TAPS):
                        for b in range(2):
                            k = 2 * i + b
                            src = Z[:, bass.ds(k, 1), j:j + S].rearrange("p a t -> p (a t)")
                            acc = tmp[:, b]
                            w = col(1, "conv_w", TAPS * k + j)
                            if j:
                                v.wait_ge(conv_tap, 2 * (TAPS - 1) * i + 2 * j + b - 1)
                            if j == 0:
                                v.tensor_scalar(acc, src, w, col(1, "conv_b", k),
                                                ALU.mult, ALU.add).then_inc(conv_tap, 1)
                            elif j < TAPS - 1:
                                v.scalar_tensor_tensor(acc, src, w, acc, ALU.mult, ALU.add).then_inc(conv_tap, 1)
                            else:
                                v.scalar_tensor_tensor(src, src, w, acc, ALU.mult, ALU.add).then_inc(conv_done, 1)

                v.wait_ge(rope_table, 3)
                link(v.tensor_scalar(SIN, SIN, const(1, "rope_s"), None, ALU.mult))
                for k in range(14):
                    v.wait_ge(swapped, k + 1)
                    v.tensor_tensor(tmp[:, k % 2], bank[2 + k % 2][:], SIN, ALU.mult).then_inc(rope_sin, 1)
                    link(v.tensor_tensor(QK[:, k], QK[:, k], COS, ALU.mult))
                    v.wait_ge(rope_sin, k + 1)
                    v.tensor_tensor(QK[:, k], QK[:, k], tmp[:, k % 2], ALU.add).then_inc(roped, 1)

                v.wait_ge(act_read, 8 + 16 + 5)
                for q in range(TT):
                    link(v.tensor_scalar(V_TOK[:, 4, q, 0:NH], V_TOK[:, 4, q, 0:NH], const(1, "cmp_valid", 1, q), None, ALU.mult))

                for m in range(2):
                    full = SCR[:, 0:16 * 124].rearrange("p (c g n) -> p c g n", c=16, g=NKV)
                    v.wait_ge(pair_keys_in, 16 * 16)
                    for j in range(16):
                        ins = v.tensor_scalar(full[:, j], X[:, 4 * m:4 * m + 4, 2 * j:2 * j + 16 * 30 + 1:16],
                                              col(1, "cmp_pos", 16 * m + j), None, ALU.add)
                    link(ins)
                    hi = HI[B].rearrange("p c t -> p (c t)")[:, 2048 * m:2048 * m + 16 * 124]
                    lo = LO[B].rearrange("p c t -> p (c t)")[:, 2048 * m:2048 * m + 16 * 124]
                    link(v.tensor_copy(hi, SCR[:, 0:16 * 124]))
                    ins = v.tensor_tensor(lo, SCR[:, 0:16 * 124], hi.bitcast(F32), ALU.subtract)
                    ins.then_inc(blocks_made, 1)
                    v.wait_ge(blocks_made, m + 1)

                v.wait_ge(mean_ready, c.add("mean"))
                for k in range(KT):
                    v.scalar_tensor_tensor(Z_OUT[:, k], bank[6][:], -1.0 / D, Z_OUT[:, k], ALU.mult, ALU.add).then_inc(centered, 1)
                variance()
                for k in range(KT):
                    v.tensor_tensor(Z_OUT[:, k], Z_OUT[:, k], stat[:, 1], ALU.mult).then_inc(centered, 1)
                split(KT, lambda k, to: None, B)

                reads, used = c["act_read"] + 8 + 16 + 5 + 8, c["dve_read"]
                with v.Fori(0, 8) as i:
                    v.wait_ge(act_read, reads + i + 1)
                    v.wait_ge(mm_done, FIRST["conv_out"] + 2 * i + 2)
                    v.scalar_tensor_tensor(Z[:, bass.ds(i, 1), TAPS - 1:].rearrange("p a t -> p (a t)"),
                                           bank[(FIRST["conv_out"] + 1) % 2][:], col(1, "b_conv_out", i),
                                           tmp[:, 2], ALU.add, ALU.mult).then_inc(dve_read, 1)
                c["act_read"] = reads + 8
                c.add("dve_read", 8)

                def maxima(n):
                    b, kw = n % 2, (n % 4 + 1) * P
                    v.wait_ge(qk_done, n + 1)
                    for j in range(2):
                        ins = v.tensor_reduce(MX[:, b, j:1 + j], bank[2 + 2 * b + j][:, 0:kw], AX.X, ALU.max)
                    link(ins)
                    v.tensor_scalar(MX[:, b, 2:4], MX[:, b, 0:2], -0.125, None, ALU.mult).then_inc(neg_ready, 1)

                def scale(n):
                    h, qt, b = n // 4, n % 4, n % 2
                    v.wait_ge(exp_done, 2 * n + 2)
                    link(v.reciprocal(SUMS[:, b, 2:4], SUMS[:, b, 0:2]))
                    link(v.tensor_tensor(SUMS[:, b, 2:4], SUMS[:, b, 2:4], V_TOK[:, 4, qt, NH + h:h + 2 * NH + 1:NH], ALU.mult))
                    for j in range(2):
                        p = tmp[:, 2 * b + j, 0:(qt + 1) * P]
                        v.tensor_scalar(p, p, SUMS[:, b, 2 + j:3 + j], None, ALU.mult).then_inc(scaled, 1)

                def keep_pt(n):
                    b, kw = n % 2, (n % 4 + 1) * P
                    v.wait_ge(tr_done, n + 1)
                    if n >= 2:
                        v.wait_ge(pv_done, n - 1)
                    v.tensor_copy(PT[:, b, 1, 0:kw], bank[1][:, 0:kw]).then_inc(pt_dve, 1)

                def per_row(x):
                    return x.unsqueeze(2).to_broadcast([P, TT, NCMP])

                def compressed_shift(h):
                    v.wait_ge(c_scores, h + 1)
                    sc = bank[6][:, 0:TT * NCMP].rearrange("p (q n) -> p q n", q=TT)
                    link(v.tensor_reduce(CST[:, 0:4], sc, AX.X, ALU.max))
                    v.tensor_tensor(PC, sc, per_row(CST[:, 0:4]), ALU.subtract).then_inc(c_shifted, 1)

                def compressed_scale(h):
                    v.wait_ge(c_exp, h + 1)
                    link(v.tensor_reduce(CST[:, 4:8], PC, AX.X, ALU.add))
                    link(v.reciprocal(CST[:, 4:8], CST[:, 4:8]))
                    link(v.tensor_tensor(CST[:, 4:8], CST[:, 4:8], V_TOK[:, 4, :, h:h + 1].rearrange("p q a -> p (q a)"), ALU.mult))
                    v.tensor_tensor(PC, PC, per_row(CST[:, 4:8]), ALU.mult).then_inc(c_scaled, 1)

                def compressed_keep(h):
                    v.wait_ge(c_tr, h + 1)
                    if h >= 2:
                        v.wait_ge(pv_done, 4 * h - 4)
                    v.tensor_copy(PCT[0:NCMP, h % 2], bank[6][0:NCMP, :]).then_inc(c_kept, 1)

                def merge(hp):
                    v.wait_ge(pv_done, 8 * hp + 8)
                    v.tensor_tensor(GA[:, hp], GA[:, hp], bank[7][:], ALU.mult).then_inc(o_read, 1)
                    v.wait_ge(o_read, hp + 1)
                    v.tensor_tensor(Z_OUT[:, hp], Z_OUT[:, hp], GA[:, hp], ALU.add).then_inc(merged, 1)
                    v.wait_ge(merged, hp + 1)
                    v.tensor_copy(HI[A][:, hp], Z_OUT[:, hp]).then_inc(hi_made, 1)
                    v.wait_ge(hi_made, c["made"] + 1)
                    v.tensor_tensor(LO[A][:, hp], Z_OUT[:, hp], HI[A][:, hp].bitcast(F32), ALU.subtract).then_inc(lo_made, 1)
                    c.add("made")

                N = NH * TT
                compressed_shift(0)
                compressed_scale(0)
                compressed_keep(0)
                for n in range(N + 3):
                    if 1 <= n <= N:
                        scale(n - 1)
                    if n < N:
                        maxima(n)
                    if 1 <= n <= N:
                        keep_pt(n - 1)
                    if n % 4 < 3 and n // 4 + 1 < NH:
                        (compressed_shift, compressed_scale, compressed_keep)[n % 4](n // 4 + 1)
                    if n >= 10 and (n - 10) % 8 == 0:
                        merge((n - 10) // 8)

                v.wait_ge(x_back, 128)
                residual_add("attn_out")
                rms_norm("g_ffn", A)
                for q in range(3):
                    gated_operands(f"ffn_up_{q}", B)
                    residual_add(f"ffn_down_{q}")
                variance()
                for k in range(KT):
                    v.scalar_tensor_tensor(X[:, k], X[:, k], col(1, "g_final", k), stat[:, 1], ALU.mult, ALU.mult).then_inc(normed, 1)

            def center():
                v.wait_ge(mean_ready, c.add("mean"))
                for k in range(KT):
                    v.scalar_tensor_tensor(X[:, k], bank[6][:], -1.0 / D, X[:, k], ALU.mult, ALU.add).then_inc(centered, 1)

            def layer_norm(gain, bias, dst=None, done=None):
                center()
                variance(1e-5)
                for k in range(KT):
                    link(v.tensor_tensor(X[:, k], X[:, k], stat[:, 1], ALU.mult))
                    ins = v.tensor_scalar(X[:, k], X[:, k], col(2, gain, k), col(2, bias, k), ALU.mult, ALU.add)
                    if dst is None:
                        ins.then_inc(done, 1)
                        continue
                    ins.then_inc(full_made, 1)
                    v.wait_ge(full_made, c.add("full"))
                    to_operand(X[:, k], dst, k)

            def to_operand(src, dst, k):
                v.tensor_copy(HI[dst][:, k], src).then_inc(hi_made, 1)
                v.wait_ge(hi_made, c.add("made"))
                v.tensor_tensor(LO[dst][:, k], src, HI[dst][:, k].bitcast(F32), ALU.subtract).then_inc(lo_made, 1)

            def squared_relu(name, dst):
                first, made, used = FIRST[name], c["made"], c["dve_read"]
                v.wait_ge(mm_done, first)
                v.wait_ge(lo_made, made)
                with v.Fori(0, 4) as i:
                    for u in range(2):
                        n = 2 * i + u
                        v.wait_ge(mm_done, first + n + 1)
                        if made + u >= 2:
                            v.wait_ge(lo_made, made + n - 1)
                        v.tensor_scalar(tmp[:, 2 + u], bank[(first + u) % 2][:], 0.0, None, ALU.max).then_inc(relu_made, 1)
                        v.wait_ge(relu_made, c["relu"] + n + 1)
                        v.tensor_tensor(stat[:, u], bank[(first + u) % 2][:], tmp[:, 2 + u], ALU.mult).then_inc(dve_read, 1)
                        v.wait_ge(dve_read, used + n + 1)
                        hi = HI[dst][:, bass.ds(n, 1), :].rearrange("p a t -> p (a t)")
                        lo = LO[dst][:, bass.ds(n, 1), :].rearrange("p a t -> p (a t)")
                        v.tensor_copy(hi, stat[:, u]).then_inc(hi_made, 1)
                        v.wait_ge(hi_made, made + n + 1)
                        v.tensor_tensor(lo, stat[:, u], hi.bitcast(F32), ALU.subtract).then_inc(lo_made, 1)
                c.add("relu", 8)
                c.add("made", 8)
                c.add("dve_read", 8)

            ALPHA = 2.0 ** 0.25

            def block_2():
                v.wait_ge(params_in, c.add("params", 32))
                v.memset(QKV[:, :, 0:PAD], 0.0).then_inc(dve_step, 1)
                v.memset(U_POOL[:, :, 0:16], 0.0).then_inc(dve_step, 1)
                v.memset(WIN[:, :, 0:16], 0.0).then_inc(gated_2, 1)
                v.wait_ge(dve_step, c.add("step", 2))
                v.wait_ge(gated_2, 1)
                layer_norm("ln_in_g", "ln_in_b", A)
                reads = c["act_read"]
                for g in range(4):
                    v.wait_ge(act_read, reads + g + 1)
                    src = U_POOL[:, g]
                    w = 1
                    for r in range(g + 1):
                        dst = WIN[:, r % 2]
                        link(v.tensor_tensor(dst[:, 16:], src[:, 16:], src[:, 16 - w:16 - w + S], ALU.add))
                        src, w = dst, 2 * w
                    link(v.tensor_tensor(src[:, 16:32], src[:, 16:32], const(2, "per_count", 16), ALU.mult) if w == 16 else
                         v.tensor_tensor(src[:, 16:16 + w], src[:, 16:16 + w], const(2, "per_count", w), ALU.mult))
                    link(v.tensor_scalar(src[:, 16 + w:], src[:, 16 + w:], 1.0 / w, None, ALU.mult))
                    link(v.tensor_tensor(WIN[:, 0, 16:], src[:, 16:], U_POOL[:, g, 16:], ALU.subtract))
                    to_operand(WIN[:, 0, 16:], B, g)
                    v.wait_ge(lo_made, c["made"])
                with v.Fori(0, 12) as i:
                    v.wait_ge(act_read, reads + 4 + 2 * i + 2)
                    v.wait_ge(conv4_done, 2 * i)
                    for j in range(4):
                        for b in range(2):
                            k = 2 * i + b
                            src = QKV[:, bass.ds(k, 1), j:j + S].rearrange("p a t -> p (a t)")
                            w = col(2, "conv_w", 4 * k + j)
                            if j:
                                v.wait_ge(conv4_tap, 6 * i + 2 * j + b - 1)
                            if j == 0:
                                v.tensor_scalar(tmp[:, b], src, w, None, ALU.mult).then_inc(conv4_tap, 1)
                            elif j < 3:
                                v.scalar_tensor_tensor(tmp[:, b], src, w, tmp[:, b], ALU.mult, ALU.add).then_inc(conv4_tap, 1)
                            else:
                                v.scalar_tensor_tensor(src, src, w, tmp[:, b], ALU.mult, ALU.add).then_inc(conv4_done, 1)
                v.wait_ge(act_read, reads + 29)
                c.add("act_read", 29)
                v.tensor_tensor(SPS, BA[:, :, 8:16], col(2, "dt_bias", 0, 8).unsqueeze(1).to_broadcast([P, TT, 8]),
                                ALU.add).then_inc(sp_in, 1)
                v.wait_ge(sp_log, 1)
                link(v.tensor_scalar(SPW, SPU, 1.0, None, ALU.add))
                link(v.tensor_scalar(SPW, SPW, -1.0, 1e-30, ALU.add, ALU.max))
                link(v.reciprocal(SPW, SPW))
                link(v.tensor_tensor(SPW, SPW, SPU, ALU.mult))
                link(v.tensor_tensor(SPL, SPL, SPW, ALU.mult))
                link(v.tensor_scalar(SPW, SPU, -0.5, 1.0, ALU.mult, ALU.add))
                link(v.tensor_tensor(SPW, SPW, SPU, ALU.mult))
                link(v.tensor_tensor(SPL, SPL, SPW, ALU.max))
                link(v.scalar_tensor_tensor(SPL, SPS, 0.0, SPL, ALU.max, ALU.add))
                v.scalar_tensor_tensor(DEC, SPL, -1.0, EXA[:, 0:1].to_broadcast([P, TT, 8]), ALU.mult, ALU.mult)\
                 .then_inc(dec_ready, 1)
                for k in range(16):
                    v.wait_ge(l2_rstd, k + 1)
                    v.scalar_tensor_tensor(QKV_T[:, k], QKV_T[:, k], P ** -0.5 if k < 8 else 1.0, tmp[:, 2 + k % 2],
                                           ALU.mult, ALU.mult).then_inc(l2_done, 1)
                v.wait_ge(gc_sum, 1)
                v.tensor_copy(GC, bank[2][:, 0:32].rearrange("p (q h) -> p q h", q=TT)).then_inc(gc_kept, 1)
                v.wait_ge(rows_tr, 1)
                v.tensor_copy(ROWS[0:8, 0], bank[3][0:8, :]).then_inc(rows_kept, 1)
                v.tensor_copy(ROWS[0:8, 1], bank[4][0:8, :]).then_inc(rows_kept, 1)
                v.tensor_tensor(EGLC, bank[5][:, 0:32].rearrange("p (q h) -> p q h", q=TT), GC, ALU.subtract).then_inc(gc_kept, 1)
                v.wait_ge(decays, 1)
                link(v.tensor_tensor(BE, BETA, EGC, ALU.mult))

                EG = stat[:, 1]

                def per_token(x, h):
                    return x[:, :, h:h + 1].to_broadcast([P, TT, P])

                def tiles(x):
                    return x.rearrange("p (q n) -> p q n", q=TT)

                def level(i):
                    return const(2, "levels", 128, 128 * i).unsqueeze(1).to_broadcast([P, TT, P])

                identities = ident.unsqueeze(1).to_broadcast([P, TT, P])

                def prepare(h, slot):
                    b = h % 2
                    if slot == 0:
                        v.wait_ge(eg_done, h + 1)
                        v.wait_ge(uw_done, h)
                        link(v.tensor_tensor(DT, tiles(bank[2]), per_token(GC, h), ALU.subtract))
                        v.scalar_tensor_tensor(DT, DT, 0.0, const(2, "mask64", 128).unsqueeze(1).to_broadcast([P, TT, P]),
                                               ALU.min, ALU.add).then_inc(arg_done, 1)
                        if h >= 2:
                            v.wait_ge(o_done, h - 1)
                        v.tensor_tensor(QG[b], QKV_T[:, h], EG, ALU.mult)
                        link(v.tensor_copy(EGL[:, b], stat[:, 1, 63:S:64]))
                        v.tensor_tensor(KBT.rearrange("p q n -> p (q n)"), QKV_T[:, 8 + h], bank[3][:], ALU.mult).then_inc(kb_done, 1)
                        v.wait_ge(tok_done, h + 1)
                        if h:
                            v.wait_ge(uw_done, h)
                        v.tensor_tensor(VB, tiles(bank[5]), per_token(BETA, h), ALU.mult).then_inc(tokv_done, 1)
                        v.tensor_tensor(KBE, tiles(bank[4]), per_token(BE, h), ALU.mult).then_inc(tokv_done, 1)
                        v.tensor_tensor(KG[b], tiles(bank[4]), per_token(EGLC, h), ALU.mult).then_inc(tokv_done, 1)
                    if slot == 1:
                        v.wait_ge(kk_done, h + 1)
                        v.wait_ge(dt_done, h + 1)
                        v.tensor_tensor(MT, tiles(bank[2]), DT, ALU.mult).then_inc(m_done, 1)
                        v.tensor_tensor(ATT[b], tiles(bank[3]), DT, ALU.mult).then_inc(m_done, 1)
                        v.wait_ge(m_done, 2 * h + 2)
                        link(v.tensor_tensor(CT, MT, level(0), ALU.mult))
                        v.tensor_tensor(UM, identities, CT, ALU.subtract).then_inc(u_ready, 1)
                        v.wait_ge(u_ready, 6 * h + 1)
                        v.tensor_tensor(CT, MT, level(1), ALU.mult).then_inc(ct_ready, 1)
                    if slot == 2:
                        v.wait_ge(t_done, h + 1)
                        v.tensor_copy(TM.rearrange("p q n -> p (q n)"), bank[4][:]).then_inc(t_ready, 1)
                        v.wait_ge(t_ready, 5 * h + 1)
                    if 3 <= slot < 8:
                        l = slot - 3
                        if l < 4:
                            v.wait_ge(x_done, 5 * h + l + 1)
                            v.tensor_tensor(CT, MT, level(l + 2), ALU.mult).then_inc(ct_ready, 1)
                        v.wait_ge(y_done, 5 * h + l + 1)
                        if l < 4:
                            v.tensor_tensor(TM, TM, tiles(bank[2]), ALU.subtract).then_inc(t_ready, 1)
                        v.tensor_tensor(UM, UM, tiles(bank[3]), ALU.subtract).then_inc(u_ready, 1)
                        v.wait_ge(u_ready, 6 * h + l + 2)
                        if l < 4:
                            v.wait_ge(t_ready, 5 * h + l + 2)
                    if slot == 8:
                        v.wait_ge(uw_done, h + 1)
                        v.tensor_copy(WT[b], bank[5][:]).then_inc(wt_ready, 1)

                def new_values(h, k):
                    r = slice(64 * (k % 2), 64 * (k % 2) + 64)
                    v.wait_ge(uv_ready, h + 1)
                    if k == 0:
                        v.wait_ge(o_done, h)
                        v.tensor_copy(VNEW[r, :], UV[h % 2][r, 0]).then_inc(vnew_ready, 1)
                    else:
                        v.wait_ge(vn_done, 7 * h + k)
                        v.tensor_tensor(VNEW[r, :], UV[h % 2][r, k // 2], bank[6][r, 0:P], ALU.subtract).then_inc(vnew_ready, 1)

                def new_state(h, k):
                    v.wait_ge(ds_done, 7 * h + k + 1)
                    if k == 0:
                        v.tensor_copy(ST, bank[7][:, 0:P]).then_inc(s_ready, 1)
                    else:
                        v.wait_ge(s_ready, 7 * h + k)
                        v.scalar_tensor_tensor(ST, ST, EGL[:, h % 2, k:k + 1], bank[7][:, 0:P], ALU.mult, ALU.add)\
                         .then_inc(s_ready, 1)

                for h in range(9):
                    for slot in range(9):
                        if h >= 1 and slot < 8:
                            new_values(h - 1, slot)
                        if h < 8:
                            prepare(h, slot)
                        if h >= 1 and slot < 7:
                            new_state(h - 1, slot)
                        if h >= 1 and slot == 8:
                            v.wait_ge(o_rstd, h)
                            v.scalar_tensor_tensor(OUT2[:, h - 1], bank[0][:], col(2, "o_norm"), tmp[:, 1],
                                                   ALU.mult, ALU.mult).then_inc(o_kept, 1)

                v.wait_ge(o_kept, 8)
                used = c["dve_read"]
                with v.Fori(0, 4) as i:
                    for u in range(2):
                        n = 2 * i + u
                        o = OUT2[:, bass.ds(n, 1), :].rearrange("p a t -> p (a t)")
                        v.wait_ge(z_gate, n + 1)
                        v.wait_ge(mm_done, FIRST["z_2"] + n + 1)
                        v.tensor_tensor(tmp[:, 2 + u], bank[(FIRST["z_2"] + u) % 2][:], tmp[:, 2 + u], ALU.mult).then_inc(dve_read, 1)
                        v.wait_ge(dve_read, used + n + 1)
                        v.tensor_tensor(o, o, tmp[:, 2 + u], ALU.mult).then_inc(gated_2, 1)
                v.wait_ge(gated_2, 9)
                reads = c["act_read"]
                with v.Fori(0, 4) as i:
                    for u in range(2):
                        n = 2 * i + u
                        o = OUT2[:, bass.ds(n, 1), :].rearrange("p a t -> p (a t)")
                        v.wait_ge(act_read, reads + n + 1)
                        v.tensor_tensor(o, o, tmp[:, 2 + u], ALU.mult).then_inc(gated_2, 1)
                v.wait_ge(gated_2, 17)
                v.wait_ge(pool_scaled, 8)
                v.wait_ge(mm_done, FIRST["z_2"])
                made = c["made"]
                with v.Fori(0, 4) as i:
                    for u in range(2):
                        n = 2 * i + u
                        o = OUT2[:, bass.ds(n, 1), :].rearrange("p a t -> p (a t)")
                        y = YA[:, bass.ds(n, 1), :].rearrange("p a t -> p (a t)")
                        hi = HI[B][:, bass.ds(n, 1), :].rearrange("p a t -> p (a t)")
                        lo = LO[B][:, bass.ds(n, 1), :].rearrange("p a t -> p (a t)")
                        v.wait_ge(act_read, reads + 8 + n + 1)
                        v.tensor_tensor(y, y, tmp[:, 2 + u], ALU.mult).then_inc(gated_2, 1)
                        v.wait_ge(gated_2, 17 + n + 1)
                        v.tensor_tensor(o, o, y, ALU.add).then_inc(full_made, 1)
                        v.wait_ge(full_made, c["full"] + n + 1)
                        v.tensor_copy(hi, o).then_inc(hi_made, 1)
                        v.wait_ge(hi_made, made + n + 1)
                        v.tensor_tensor(lo, o, hi.bitcast(F32), ALU.subtract).then_inc(lo_made, 1)
                c.add("full", 8)
                c.add("made", 8)
                c.add("act_read", 16)
                c.add("dve_read", 8)
                residual_add("w_out_2", ALPHA)
                layer_norm("ln1_g", "ln1_b", A)
                for q in range(4):
                    squared_relu(f"up_{q}_2", B)
                    residual_add(f"down_{q}_2", ALPHA if q == 0 else None)
                embed(2)
                layer_norm("ln2_g", "ln2_b", None, normed)

            def embed(b):
                if b == 2:
                    v.wait_ge(dve_read, c["dve_read"])
                    for k in range(KT):
                        to_operand(X[:, k], A, k)
                v.wait_ge(p_in, 16 * (1 if b == 2 or 2 not in blocks else 2))
                v.wait_ge(mm_done, FIRST[f"ple_{b}"])
                for k in range(2):
                    to_operand(tmp[:, k] if b == 2 else P3[:, k], B, k)
                first, reads, used, added = FIRST[f"ple_{b}"], c["act_read"], c["dve_read"], c["added"]
                with v.Fori(0, 8) as i:
                    v.wait_ge(act_read, reads + i + 1)
                    v.wait_ge(mm_done, first + 2 * i + 2)
                    v.wait_ge(x_added, added + i)
                    v.tensor_tensor(tmp[:, 3], bank[(first + 1) % 2][:], tmp[:, 2], ALU.mult).then_inc(dve_read, 1)
                    v.wait_ge(dve_read, used + i + 1)
                    x = X[:, bass.ds(i, 1), :].rearrange("p a t -> p (a t)")
                    v.tensor_tensor(x, x, tmp[:, 3], ALU.add).then_inc(x_added, 1)
                c.add("act_read", 8)
                c.add("dve_read", 8)
                c.add("added", 8)

            def block_3():
                v.wait_ge(params_in, c.add("params", 32))
                v.memset(SC[:, 0, :], NEG).then_inc(rel_fill, 1)
                rms_norm("g_mix", A, 3)
                v.wait_ge(bias_sum, 1)
                v.memset(SC[:, 0, 0:P], NEG).then_inc(rel_fill, 1)
                reads = c["act_read"]
                v.wait_ge(act_read, reads + 12)
                v.tensor_scalar(QKB[:, 0:4], QKB[:, 0:4], 0.125, None, ALU.mult).then_inc(q_scaled, 1)
                v.tensor_scalar(QKB[:, 8:12], QKB[:, 8:12], 0.125, None, ALU.mult).then_inc(q_scaled, 1)
                c.add("act_read", 18)

                def softplus(m):
                    h, st = m // 4, 3 - m % 4
                    w = S - P * st
                    v.wait_ge(sp_ready, m + 1)
                    v.wait_ge(suffixed, max(4 * (h - 1), 0))
                    link(v.scalar_tensor_tensor(LS[:, h % 2, st, 0:w], bank[2 + m % 4][:, 0:w], 0.0, stat[:, m % 2, 0:w],
                                                ALU.max, ALU.add))
                    v.tensor_tensor(LS[:, h % 2, st, 0:P], LS[:, h % 2, st, 0:P], const(3, "strict", 128), ALU.mult)\
                     .then_inc(l_ready, 1)

                v.wait_ge(mm_done, FIRST["qk_3"])
                v.wait_ge(bias_turned, 4)
                for m in range(32 + 3):
                    if m < 32:
                        softplus(m)
                    if m >= 10 and (m - 10) % 8 == 0:
                        p = (m - 10) // 8
                        v.wait_ge(pv3_done, 8 * p + 8)
                        to_operand(bank[6 + p % 2][:], B, p)

                def window_scores(h):
                    v.wait_ge(sw_qk, h + 1)
                    v.wait_ge(sw_exp, h)
                    v.tensor_tensor(SC[:, 0, P:], bank[2][:, P:256], BIAS[:, h, P:], ALU.add)
                    v.tensor_tensor(SC[:, 1], bank[2][:, 256:512], BIAS[:, h], ALU.add)
                    link(v.tensor_tensor(SC[:, 2:4], bank[3].rearrange("p (n k) -> p n k", n=2),
                                         BIAS[:, h:h + 1].to_broadcast([P, 2, 256]), ALU.add))
                    link(v.tensor_reduce(SW[:, 0], SC, AX.X, ALU.max))
                    link(v.tensor_scalar(SW[:, 0], SW[:, 0], col(3, "sinks", h), None, ALU.max))
                    link(v.tensor_scalar(SW[:, 1], SW[:, 0], -1.0, None, ALU.mult))
                    v.tensor_scalar(SW[:, 2], SW[:, 1], col(3, "sinks", h), None, ALU.add).then_inc(sw_neg, 1)

                def window_scale(h):
                    v.wait_ge(sw_exp, h + 1)
                    link(v.tensor_tensor(SW[:, 5], SW[:, 3], SW[:, 4], ALU.add))
                    link(v.reciprocal(SW[:, 5], SW[:, 5]))
                    for n in range(TT):
                        lo = P if n == 0 else 0
                        ins = v.tensor_scalar(PB[:, n, lo:], PB[:, n, lo:], SW[:, 5, n:n + 1], None, ALU.mult)
                    ins.then_inc(sw_scaled, 1)

                def window_pt(h):
                    v.wait_ge(sw_tr, h + 1)
                    v.wait_ge(sw_pv, h)
                    v.tensor_copy(PTB.rearrange("p n k -> p (n k)")[:, 512:], bank[5][:]).then_inc(sw_pt_dve, 1)

                v.wait_ge(bias_placed, 4)
                v.wait_ge(rel_fill, 2)
                for h in range(9):
                    if h < 8:
                        window_scores(h)
                    if h >= 1:
                        window_pt(h - 1)
                    if h < 8:
                        window_scale(h)
                    if h and h % 2 == 0:
                        v.wait_ge(sw_pv, h)
                        to_operand(bank[6 + (h - 1) // 2 % 2][:], B, 4 + (h - 1) // 2)

                v.wait_ge(act_read, c.add("act_read", 16))
                first, made, full, used = FIRST["up_3"], c["made"], c["full"], c["dve_read"]
                with v.Fori(0, 4) as i:
                    for u in range(2):
                        n, s = 2 * i + u, (first + u) % 2
                        ga = GATE_A[:, bass.ds(n, 1), :].rearrange("p a t -> p (a t)")
                        gb = GATE_B[:, bass.ds(n, 1), :].rearrange("p a t -> p (a t)")
                        hi = HI[A][:, bass.ds(n, 1), :].rearrange("p a t -> p (a t)")
                        lo = LO[A][:, bass.ds(n, 1), :].rearrange("p a t -> p (a t)")
                        v.wait_ge(mm_done, first + n + 1)
                        v.wait_ge(lo_made, made + n - 1)
                        v.tensor_tensor(tmp[:, u], bank[s][:], ga, ALU.mult)
                        v.tensor_tensor(tmp[:, 2 + u], bank[2 + s][:], gb, ALU.mult).then_inc(dve_read, 1)
                        v.wait_ge(dve_read, used + n + 1)
                        v.tensor_tensor(tmp[:, u], tmp[:, u], tmp[:, 2 + u], ALU.add).then_inc(full_made, 1)
                        v.wait_ge(full_made, full + n + 1)
                        v.tensor_copy(hi, tmp[:, u]).then_inc(hi_made, 1)
                        v.wait_ge(hi_made, made + n + 1)
                        v.tensor_tensor(lo, tmp[:, u], hi.bitcast(F32), ALU.subtract).then_inc(lo_made, 1)
                c.add("made", 8)
                c.add("full", 8)
                c.add("dve_read", 8)
                residual_add("w_o_3")
                rms_norm("g_mlp", A, 3)
                for q in range(4):
                    squared_relu(f"up_{q}_3", B)
                    residual_add(f"down_{q}_3")
                rms_norm("g_pe", A, 3)
                embed(3)
                variance()
                for k in range(KT):
                    v.scalar_tensor_tensor(X[:, k], X[:, k], col(3, "g_final", k), stat[:, 1], ALU.mult, ALU.mult).then_inc(normed, 1)

            v.wait_ge(x_in, 16)
            for b in blocks:
                {1: block_1, 2: block_2, 3: block_3}[b]()

        @block.tensor
        def _(pe):
            c = Count()

            def three(o, l_hi, l_lo, r_hi, r_lo, start, stop):
                pe.matmul(o, l_hi, r_hi, start=start, stop=False)
                pe.matmul(o, l_hi, r_lo, start=False, stop=False)
                return pe.matmul(o, l_lo, r_hi, start=False, stop=stop)

            def sum_squares():
                for k in range(KT):
                    pe.wait_ge(sq_ready, c.add("sq"))
                    pe.matmul(bank[7][:], ones, tmp[:, k % 2], start=k == 0, stop=k == KT - 1).then_inc(sq_summed, 1)

            def unit(U, s, dst, nk=KT, made=None):
                pe.wait_ge(w_lo_ready, U + 1)
                for k in range(nk):
                    if made is not None:
                        pe.wait_ge(lo_made, made + k + 1)
                    ins = three(bank[s][:], w_hi[:, s, k], w_lo[:, s, k], HI[dst][:, k], LO[dst][:, k], k == 0, k == nk - 1)
                ins.then_inc(mm_done, 1)

            def banks_free():
                pe.wait_ge(act_read, c["act_read"])
                pe.wait_ge(dve_read, c["dve_read"])

            def single(name, reader, dst, nk=KT, fresh=False):
                first, key = FIRST[name], "act_read" if reader is act_read else "dve_read"
                base = c[key]
                banks_free()
                with pe.Fori(0, COUNT[name] // 2) as i:
                    for u in range(2):
                        pe.wait_ge(reader, base + 2 * i + (u - 1 if base + u else 0))
                        unit(first + 2 * i + u, (first + u) % 2, dst, nk, c["made"] if fresh and u == 0 else None)
                c.add(key, COUNT[name])
                if fresh:
                    c.add("made", nk)

            def pairs(name, even=0, odd=0, fresh=None):
                first = FIRST[name]
                abase, dbase = c["act_read"], c["dve_read"]
                banks_free()
                with pe.Fori(0, COUNT[name] // 2) as i:
                    pe.wait_ge(act_read, abase + i)
                    unit(first + 2 * i, first % 2, even, made=c["made"] if fresh == even else None)
                    pe.wait_ge(dve_read, dbase + i)
                    unit(first + 2 * i + 1, (first + 1) % 2, odd, made=c["made"] if fresh == odd != even else None)
                c.add("act_read", COUNT[name] // 2)
                c.add("dve_read", COUNT[name] // 2)
                if fresh is not None:
                    c.add("made", KT)

            def block_1():
                pe.wait_ge(params_in, c.add("params", 16 * 5))
                sum_squares()
                pairs("conv_gate", fresh=A)
                single("qk", act_read, A)
                banks_free()
                for k in range(5):
                    U = FIRST["token_major"] + k
                    s = U % 2
                    pe.wait_ge(w_lo_ready, U + 1)
                    pe.wait_ge(act_read, c["act_read"] + max(k - 1, 0))
                    for q in range(TT):
                        tok = slice(q * P, q * P + P)
                        for kt in range(KT):
                            ins = three(bank[s][:, tok], HI[A][:, kt, tok], LO[A][:, kt, tok], w_hi[:, s, kt], w_lo[:, s, kt],
                                        kt == 0, kt == KT - 1)
                    ins.then_inc(mm_done, 1)
                c.add("act_read", 5)
                for k in range(14):
                    if k >= 2:
                        pe.wait_ge(roped, k - 1)
                    pe.matmul(bank[2 + k % 2][:], const(1, "swap", 128), QK[:, k], start=True, stop=True).then_inc(swapped, 1)

                pe.wait_ge(roped, 14)
                for k in range(8):
                    U = FIRST["compress"] + k
                    s, m, half = U % 2, k // 4, k % 2
                    pe.wait_ge(w_lo_ready, U + 1)
                    pe.wait_ge(blocks_made, m + 1)
                    for kt in range(KT):
                        at_c = 2048 * m + (8 * half + kt) * 124
                        hi = HI[B].rearrange("p c t -> p (c t)")[:, at_c:at_c + 124]
                        lo = LO[B].rearrange("p c t -> p (c t)")[:, at_c:at_c + 124]
                        ins = three(bank[2 + k // 2][:, 0:124], w_hi[:, s, kt], w_lo[:, s, kt], hi, lo,
                                    half == 0 and kt == 0, half == 1 and kt == KT - 1)
                    ins.then_inc(mm_done, 1)
                pe.wait_ge(hidden_ready, 2)
                for mt in range(2):
                    ins = pe.matmul(bank[6][:, 0:124], CW2K[:, mt], HID[:, 0, mt], start=mt == 0, stop=mt == 1)
                ins.then_inc(cmp_sum, 1)
                pe.wait_ge(hidden_ready, 4)
                for g in range(NKV):
                    for mt in range(2):
                        ins = pe.matmul(bank[7][0:NCMP, g * DH:(g + 1) * DH], HID[:, 1, mt, g * NCMP:(g + 1) * NCMP], CW2V[:, mt],
                                        start=mt == 0, stop=mt == 1)
                ins.then_inc(cmp_sum, 1)
                single("attn_gate", act_read, A)

                pe.wait_ge(cmp_ready, 2)
                for k in range(KT):
                    pe.wait_ge(conv_done, KT)
                    ins = pe.matmul(bank[6][:], ones, Z_OUT[:, k], start=k == 0, stop=k == KT - 1)
                ins.then_inc(mean_ready, 1)
                sum_squares()
                pairs("conv_out", A, B, fresh=B)

                def scores(n):
                    h, qt, b = n // 4, n % 4, n % 2
                    g, half = h // GROUP, slice((h % 2) * DH, (h % 2) * DH + DH)
                    q = QK[half, h // 2, qt * P:qt * P + P]
                    kw = (qt + 1) * P
                    if n >= 2:
                        pe.wait_ge(exp_done, 2 * n - 2)
                    for j, keys in enumerate((K_SEL, K_WIN)):
                        o = bank[2 + 2 * b + j]
                        pe.matmul(o[:, 0:kw], q, keys[half, g, 0:kw], start=True, stop=False)
                        ins = pe.matmul(o[:, kw - P:kw], ident, const(1, "causal", 128), start=False, stop=True)
                    ins.then_inc(qk_done, 1)

                def compressed_scores(h):
                    g, half = h // GROUP, slice((h % 2) * DH, (h % 2) * DH + DH)
                    if h:
                        pe.wait_ge(c_kept, h)
                    pe.matmul(bank[6][:, 0:TT * NCMP], ident, const(1, "cmp_mask", TT * NCMP), start=True, stop=False,
                              skip_group_check=True)
                    for qt in range(TT):
                        ins = pe.matmul(bank[6][:, qt * NCMP:(qt + 1) * NCMP], QK[half, h // 2, qt * P:qt * P + P],
                                        KC_T[half, g * NCMP:(g + 1) * NCMP], start=False, stop=qt == TT - 1, skip_group_check=True)
                    ins.then_inc(c_scores, 1)

                def compressed_transposes(h):
                    pe.wait_ge(c_scaled, h + 1)
                    for qt in range(TT):
                        ins = pe.transpose(bank[6][0:NCMP, qt * P:qt * P + P], PC[:, qt], ident)
                    ins.then_inc(c_tr, 1)

                def transposes(n):
                    qt, b = n % 4, n % 2
                    pe.wait_ge(scaled, 2 * n + 2)
                    if n >= 1:
                        pe.wait_ge(pt_act, n)
                        pe.wait_ge(pt_dve, n)
                    for j in range(2):
                        for k in range(qt + 1):
                            ins = pe.transpose(bank[j][:, k * P:k * P + P], tmp[:, 2 * b + j, k * P:k * P + P], ident)
                    ins.then_inc(tr_done, 1)

                def values(n):
                    h, qt, b = n // 4, n % 4, n % 2
                    g = h // GROUP
                    pe.wait_ge(pt_act, n + 1)
                    pe.wait_ge(pt_dve, n + 1)
                    pe.wait_ge(c_kept, h + 1)
                    if n % 8 == 0 and n:
                        pe.wait_ge(o_read, n // 8)
                    o = bank[7][(h % 2) * DH:(h % 2) * DH + DH, qt * P:qt * P + P]
                    pe.matmul(o, VC_T[0:NCMP, g * DH:(g + 1) * DH], PCT[0:NCMP, h % 2, qt * P:qt * P + P], start=True, stop=False)
                    for j in range(2):
                        for k in range(qt + 1):
                            ins = pe.matmul(o, V_TOK[:, 2 * j + g // 2, k, (g % 2) * DH:(g % 2) * DH + DH],
                                            PT[:, b, j, k * P:k * P + P], start=False, stop=j == 1 and k == qt)
                    ins.then_inc(pv_done, 1)

                banks_free()
                pe.wait_ge(keys_in, 16 * 16)
                N = NH * TT
                compressed_scores(0)
                compressed_transposes(0)
                for n in range(N + 2):
                    if n < N:
                        scores(n)
                    if n % 4 == 0 and n // 4 + 1 < NH:
                        compressed_scores(n // 4 + 1)
                    if n % 4 == 2 and n // 4 + 1 < NH:
                        compressed_transposes(n // 4 + 1)
                    if 1 <= n <= N:
                        transposes(n - 1)
                    if n >= 2:
                        values(n - 2)
                single("attn_out", dve_read, A, fresh=True)
                sum_squares()
                for q in range(3):
                    pairs(f"ffn_up_{q}", fresh=A if q == 0 else None)
                    single(f"ffn_down_{q}", dve_read, B, COUNT[f"ffn_up_{q}"] // 2, fresh=True)
                sum_squares()

            def mean(ready):
                for k in range(KT):
                    ready(k)
                    ins = pe.matmul(bank[6][:], ones, X[:, k], start=k == 0, stop=k == KT - 1)
                ins.then_inc(mean_ready, 1)

            def token_major(name, n):
                for k in range(n):
                    U = FIRST[name] + k
                    s = U % 2
                    pe.wait_ge(w_lo_ready, U + 1)
                    pe.wait_ge(act_read, c["act_read"] + max(k - 1, 0))
                    for q in range(TT):
                        tok = slice(q * P, q * P + P)
                        for kt in range(KT):
                            ins = three(bank[s][:, tok], HI[A][:, kt, tok], LO[A][:, kt, tok], w_hi[:, s, kt], w_lo[:, s, kt],
                                        kt == 0, kt == KT - 1)
                    ins.then_inc(mm_done, 1)
                c.add("act_read", n)

            def made(n):
                pe.wait_ge(lo_made, c.add("made", n))

            def embed(b):
                if b == 2:
                    c.add("made", KT)
                made(2)
                first = FIRST[f"ple_{b}"]
                abase, dbase = c["act_read"], c["dve_read"]
                banks_free()
                with pe.Fori(0, 8) as i:
                    pe.wait_ge(act_read, abase + i)
                    unit(first + 2 * i, first % 2, A)
                    pe.wait_ge(dve_read, dbase + i)
                    unit(first + 2 * i + 1, (first + 1) % 2, B, 2)
                c.add("act_read", 8)
                c.add("dve_read", 8)
                c.add("added", 8)

            def block_2():
                pe.wait_ge(params_in, c.add("params", 32))
                if 1 in blocks:
                    pe.wait_ge(normed, 8)
                mean(lambda k: None)
                sum_squares()
                single("pool_in", act_read, A, fresh=True)
                single("qkv", act_read, A)
                banks_free()
                token_major("beta_a", 1)
                for k in range(16):
                    pe.wait_ge(l2_sq, k + 1)
                    if k >= 2:
                        pe.wait_ge(l2_rstd, k - 1)
                    pe.matmul(bank[6 + k % 2][:], ones, tmp[:, k % 2], start=True, stop=True).then_inc(l2_sum, 1)
                pe.wait_ge(dec_ready, 1)
                dec = HT[:, 1].rearrange("p q h -> p (q h)")
                pe.matmul(bank[2][:, 0:32], const(2, "sum64", 128), dec, start=True, stop=True).then_inc(gc_sum, 1)
                pe.wait_ge(gc_kept, 1)
                for q in range(TT):
                    pe.transpose(bank[3][0:8, q * P:q * P + P], GC[:, q], ident)
                    pe.transpose(bank[4][0:8, q * P:q * P + P], BETA[:, q], ident)
                pe.matmul(bank[5][:, 0:32], const(2, "last64", 128), HT[:, 2].rearrange("p q h -> p (q h)"),
                          start=True, stop=True).then_inc(rows_tr, 1)
                pe.wait_ge(rows_kept, 2)

                def prepare(h, slot):
                    b = h % 2
                    q, k, val = QKV_T[:, h], QKV_T[:, 8 + h], QKV_T[:, 16 + h]
                    quad = [slice(p * P, p * P + P) for p in range(TT)]
                    if slot == 0:
                        pe.wait_ge(u_ready, 6 * h)
                        pe.wait_ge(gc_kept, 2)
                        row = ident[0:8, h:h + 1].to_broadcast([8, P])
                        pe.matmul(bank[2][:], row, ROWS[0:8, 0], start=True, stop=True)
                        pe.matmul(bank[3][:], row, ROWS[0:8, 1], start=True, stop=True).then_inc(rows_done, 1)
                        pe.wait_ge(uv_ready, h)
                        pe.wait_ge(wt_ready, h)
                        for p in range(TT):
                            pe.transpose(bank[4][:, quad[p]], k[:, quad[p]], ident)
                        for p in range(TT):
                            ins = pe.transpose(bank[5][:, quad[p]], val[:, quad[p]], ident)
                        ins.then_inc(tok_done, 1)
                    if slot == 1:
                        pe.wait_ge(kb_done, h + 1)
                        for p in range(TT):
                            pe.matmul(bank[2][:, quad[p]], k[:, quad[p]], KBT[:, p], start=True, stop=True)
                        for p in range(TT):
                            ins = pe.matmul(bank[3][:, quad[p]], k[:, quad[p]], q[:, quad[p]], start=True, stop=True)
                        ins.then_inc(kk_done, 1)
                    if slot == 2:
                        pe.wait_ge(u_ready, 6 * h + 1)
                        pe.wait_ge(tokv_done, 3 * h + 3)
                        for p in range(TT):
                            ins = pe.transpose(bank[4][:, quad[p]], UM[:, p], ident)
                        ins.then_inc(t_done, 1)
                    if 3 <= slot < 8:
                        l = slot - 3
                        pe.wait_ge(ct_ready, 5 * h + l + 1)
                        pe.wait_ge(t_ready, 5 * h + l + 1)
                        for p in range(TT):
                            ins = pe.matmul(bank[5][:, quad[p]], CT[:, p], TM[:, p], start=True, stop=True)
                        ins.then_inc(x_done, 1)
                        pe.wait_ge(x_kept, 5 * h + l + 1)
                        pe.wait_ge(u_ready, 6 * h + l + 1)
                        pe.wait_ge(m_done, 2 * h + 2)
                        for p in range(TT):
                            if l < 4:
                                pe.matmul(bank[2][:, quad[p]], UM[:, p], XM[:, p], start=True, stop=True)
                        for p in range(TT):
                            ins = pe.matmul(bank[3][:, quad[p]], XM[:, p], UM[:, p], start=True, stop=True)
                        ins.then_inc(y_done, 1)
                    if slot == 8:
                        pe.wait_ge(u_ready, 6 * h + 6)
                        for p in range(TT):
                            pe.matmul(bank[4][:, quad[p]], UM[:, p], VB[:, p], start=True, stop=True)
                        for p in range(TT):
                            ins = pe.matmul(bank[5][:, quad[p]], KBE[:, p], UM[:, p], start=True, stop=True)
                        ins.then_inc(uw_done, 1)

                def old_values(h, k):
                    r = slice(64 * (k % 2), 64 * (k % 2) + 64)
                    pe.wait_ge(wt_ready, h + 1)
                    if k:
                        pe.wait_ge(s_ready, 7 * h + k)
                        pe.matmul(bank[6][r, 0:P], WT[h % 2][:, 64 * k:64 * k + 64], ST, start=True, stop=True).then_inc(vn_done, 1)

                def outputs(h, k):
                    r = slice(64 * (k % 2), 64 * (k % 2) + 64)
                    o = bank[0][:, 64 * k:64 * k + 64]
                    if k == 0:
                        pe.wait_ge(o_kept, h)
                        pe.wait_ge(act_read, c["act_read"])
                    else:
                        pe.matmul(o, ST, QG[h % 2][:, 64 * k:64 * k + 64], start=True, stop=False)
                    pe.wait_ge(vnew_ready, 8 * h + k + 1)
                    ins = pe.matmul(o, VNEW[r, :], ATT[h % 2][r, k // 2, r], start=k == 0, stop=True)
                    if k < 7:
                        pe.matmul(bank[7][:, 0:P], KG[h % 2][r, k // 2], VNEW[r, :], start=True, stop=True).then_inc(ds_done, 1)
                    else:
                        ins.then_inc(o_done, 1)

                for h in range(9):
                    for slot in range(9):
                        if h >= 1 and slot < 8:
                            old_values(h - 1, slot)
                        if h < 8:
                            prepare(h, slot)
                        if h >= 1 and slot < 8:
                            outputs(h - 1, slot)
                        if h >= 1 and slot == 8:
                            pe.wait_ge(o_sq, h)
                            pe.matmul(bank[1][:], ones, tmp[:, 0], start=True, stop=True).then_inc(o_sum, 1)

                U = FIRST["pool_w"]
                pe.wait_ge(w_lo_ready, U + 1)
                made(4)
                for j in range(KT):
                    if j >= 2:
                        pe.wait_ge(pool_scaled, j - 1)
                    ins = three(bank[2 + j % 2][:], w_hi[:, U % 2, j], w_lo[:, U % 2, j], HI[B][:, j // 2], LO[B][:, j // 2], True, True)
                    ins.then_inc(pooled_mm if j < KT - 1 else mm_done, 1)

                pe.wait_ge(o_kept, 8)
                first, base = FIRST["z_2"], c["dve_read"]
                with pe.Fori(0, 4) as i:
                    for u in range(2):
                        pe.wait_ge(dve_read, base + 2 * i + (u - 1 if base + u else 0))
                        unit(first + 2 * i + u, (first + u) % 2, A)
                c.add("dve_read", 8)
                single("gate_b_2", act_read, A)
                single("gate_a_2", act_read, A)
                single("w_out_2", dve_read, B, fresh=True)
                mean(lambda k: pe.wait_ge(dve_read, c["dve_read"] - 7 + k))
                sum_squares()
                for q in range(4):
                    single(f"up_{q}_2", dve_read, A, fresh=q == 0)
                    single(f"down_{q}_2", dve_read, B, fresh=True)
                embed(2)
                mean(lambda k: pe.wait_ge(x_added, c["added"] - 7 + k))
                sum_squares()

            def block_3():
                pe.wait_ge(params_in, c.add("params", 32))
                pe.wait_ge(normed, 8 * (len(blocks) - 1))
                sum_squares()
                pe.wait_ge(rel_in, 32)
                pe.wait_ge(rel_fill, 1)
                pe.matmul(bank[5][0:8, 0:384], REL[0:33], HOT[0:33], start=True, stop=True).then_inc(bias_sum, 1)
                single("qk_3", act_read, A, fresh=True)
                pe.wait_ge(bias_in, 16)
                pe.wait_ge(bias_kept, 1)
                for k in range(4):
                    pe.matmul(bank[2 + k][:], const(3, "turn", 128), BIAS_T[:, 2 * k:2 * k + 2], start=True, stop=True)\
                      .then_inc(bias_turned, 1)
                banks_free()
                U = FIRST["kb_3"]
                unit(U, U % 2, A)
                c.add("act_read", 1)
                banks_free()
                token_major("v_3", 5)

                def scores(m):
                    h, st = m // 4, 3 - m % 4
                    half, ch = slice((h % 2) * DH, (h % 2) * DH + DH), h // 2
                    if m >= 4:
                        pe.wait_ge(a_ready, m - 3)
                    pe.matmul(bank[2 + m % 4][:, 0:S - P * st], QKB[half, 4 + ch, st * P:st * P + P], QKB[half, ch, st * P:],
                              start=True, stop=False, skip_group_check=True).then_inc(z_ready, 1)

                def suffix(m):
                    h, st = m // 4, 3 - m % 4
                    o, w = bank[2 + m % 4], S - P * st
                    pe.wait_ge(l_ready, m + 1)
                    pe.matmul(o[:, 0:P], ident, const(3, "mask_t", 128), start=False, stop=False, skip_group_check=True)
                    ins = pe.matmul(o[:, 0:w], const(3, "minus_sum", 128), LS[:, h % 2, st, 0:w], start=False, stop=st == 3,
                                    skip_group_check=True)
                    for later in range(st + 1, TT):
                        ins = pe.matmul(o[:, (later - st) * P:w], const(3, "minus_ones", 128), LS[:, h % 2, later, 0:S - P * later],
                                        start=False, stop=later == TT - 1, skip_group_check=True)
                    ins.then_inc(suffixed, 1)

                def values(m):
                    h, st = m // 4, 3 - m % 4
                    if m % 8 == 0:
                        pe.wait_ge(lo_made, c["made"] + max(h // 2 - 1, 0))
                    pe.wait_ge(a_ready, m + 1)
                    o = bank[6 + h // 2 % 2][(h % 2) * DH:(h % 2) * DH + DH, st * P:]
                    pe.matmul(o, V3[:, h // 2, st, (h % 2) * DH:(h % 2) * DH + DH], tmp[:, m % 4, 0:S - P * st],
                              start=st == 3, stop=st == 0, skip_group_check=True).then_inc(pv3_done, 1)

                banks_free()
                pe.wait_ge(q_scaled, 2)
                pe.wait_ge(bias_placed, 4)
                for m in range(34):
                    if m < 32:
                        scores(m)
                    if 1 <= m <= 32:
                        suffix(m - 1)
                    if m >= 2:
                        values(m - 2)
                made(4)

                def window_scores(h):
                    half, g = slice((h % 2) * DH, (h % 2) * DH + DH), h // 4
                    pe.wait_ge(sw_neg, h)
                    for n in range(TT):
                        lo = P if n == 0 else 0
                        ins = pe.matmul(bank[2 + n // 2][:, (n % 2) * 256 + lo:(n % 2) * 256 + 256],
                                        QKB[half, 8 + h // 2, n * P:n * P + P], KBD[half, g, (n - 1) * P + lo:(n + 1) * P],
                                        start=True, stop=True)
                    ins.then_inc(sw_qk, 1)

                def window_transposes(h):
                    pe.wait_ge(sw_scaled, h + 1)
                    pe.wait_ge(sw_pt_act, h)
                    pe.wait_ge(sw_pt_dve, h)
                    for n in range(TT):
                        for j in range(1 if n == 0 else 0, 2):
                            at = (n % 2) * 256 + j * P
                            ins = pe.transpose(bank[4 + n // 2][:, at:at + P], PB[:, n, j * P:j * P + P], ident)
                    ins.then_inc(sw_tr, 1)

                def window_values(h):
                    pe.wait_ge(sw_pt_act, h + 1)
                    pe.wait_ge(sw_pt_dve, h + 1)
                    if h % 2 == 0 and h >= 4:
                        pe.wait_ge(lo_made, c["made"] + h // 2 - 1)
                    half = slice((h % 2) * DH, (h % 2) * DH + DH)
                    for n in range(TT):
                        o = bank[6 + h // 2 % 2][half, n * P:n * P + P]
                        for j in range(1 if n == 0 else 0, 2):
                            ins = pe.matmul(o, V3[:, 4, n - 1 + j, (h // 4) * DH:(h // 4) * DH + DH], PTB[:, n, j * P:j * P + P],
                                            start=j == (1 if n == 0 else 0), stop=j == 1)
                    ins.then_inc(sw_pv, 1)

                pe.wait_ge(kb_in, 64)
                pe.wait_ge(a_ready, 32)
                for h in range(9):
                    if h < 8:
                        window_scores(h)
                    if h >= 1:
                        window_transposes(h - 1)
                        window_values(h - 1)
                single("gate_a_3", act_read, A)
                single("gate_b_3", act_read, A)
                made(4)
                first, base = FIRST["up_3"], c["dve_read"]
                banks_free()
                with pe.Fori(0, 4) as i:
                    for u in range(2):
                        U, s = first + 2 * i + u, (first + u) % 2
                        pe.wait_ge(dve_read, base + 2 * i + (u - 1 if base + u else 0))
                        pe.wait_ge(w_lo_ready, U + 1)
                        for k in range(KT):
                            ins = three(bank[s if k < 4 else 2 + s][:], w_hi[:, s, k], w_lo[:, s, k], HI[B][:, k], LO[B][:, k],
                                        k % 4 == 0, k % 4 == 3)
                        ins.then_inc(mm_done, 1)
                c.add("dve_read", 8)
                single("w_o_3", dve_read, A, fresh=True)
                sum_squares()
                for q in range(4):
                    single(f"up_{q}_3", dve_read, A, fresh=q == 0)
                    single(f"down_{q}_3", dve_read, B, fresh=True)
                sum_squares()
                made(KT)
                embed(3)
                sum_squares()

            pe.wait_ge(x_in, 16)
            for b in blocks:
                {1: block_1, 2: block_2, 3: block_3}[b]()


def units(w):
    K, N = w.shape
    n = -(-N // P)
    u = np.zeros((n, P, KT, P), np.float32)
    w = np.pad(w, ((0, 0), (0, n * P - N)))
    u[:, :, 0:K // P] = w.reshape(K // P, P, n, P).transpose(2, 1, 0, 3)
    return u.reshape(n, P, KT * P)


def interleave(*parts):
    return np.stack(parts, 1).reshape(-1, P, KT * P)


def vec(v):
    return np.asarray(v).reshape(-1, P).T


def stream_1(z):
    w = z["w_in"]
    edges = np.cumsum([0] + [NH * DH] + [NKV * DH] * 6 + [3 * NH] + [D] * 4)
    q, kc, vc, ks, vs, kw, vw, ng, ua, ub, ga, gc = [units(w[:, a:b]) for a, b in zip(edges[:-1], edges[1:])]
    parts = [interleave(ub, ua), q, ks, kw, kc, vc, vs, vw, ng]
    for w1 in (z["cmp_k_w1"], z["cmp_v_w1"]):
        parts.append(interleave(units(w1[0:D]), units(w1[D:2 * D])))
    parts += [ga, interleave(gc, units(z["w_conv_out"])), units(z["w_out"])]
    for a, b in ((0, D), (D, 2 * D), (2 * D, DFF1)):
        parts.append(interleave(units(z["w_ffn_gate"][:, a:b]), units(z["w_ffn_up"][:, a:b])))
        parts.append(units(z["w_ffn_down"][a:b]))
    return parts


def stream_2(z):
    w = z["w_in_2"][0]
    edges = np.cumsum([0, D // 2, 3 * D, D, 16, D, D])
    pool, qkv, gz, ba, ga, gb = [units(w[:, a:b]) for a, b in zip(edges[:-1], edges[1:])]
    pw = z["pool_w_2"][0].reshape(4, P, 2, P).transpose(1, 0, 2, 3).reshape(1, P, KT * P)
    parts = [pool, qkv, ba, pw, gz, gb, ga, units(z["w_out_2"][0])]
    for q in range(4):
        parts += [units(z["w_up_2"][0][:, q * D:(q + 1) * D]), units(z["w_down_2"][0][q * D:(q + 1) * D])]
    parts.append(interleave(units(z["ple_gate_w_2"][0]), units(z["ple_proj_w_2"][0])))
    return parts


def stream_3(z):
    w = z["w_in_3"][0]
    edges = np.cumsum([0, 512, 512, 512, 512, 128, 128, D, D])
    qa, ka, va, qb, kb, vb, ga, gb = [units(w[:, a:b]) for a, b in zip(edges[:-1], edges[1:])]
    up = units(np.concatenate([z["w_up_a_3"][0], z["w_up_b_3"][0]]))
    parts = [qa, ka, qb, kb, va, vb, ga, gb, up, units(z["w_o_3"][0])]
    for q in range(4):
        parts += [units(z["w_ff1_3"][0][:, q * D:(q + 1) * D]), units(z["w_ff2_3"][0][q * D:(q + 1) * D])]
    parts.append(interleave(units(z["w_pg_3"][0]), units(z["w_pe_3"][0])))
    return parts


def columns(z):
    c = np.zeros((3, P, N_COLS), np.float32)

    def put(block, name, a, i=0):
        at = COLS[block][0][name] + i
        c[block - 1, :, at:at + a.shape[1]] = a

    for name, key in (("g_mix", "norm_mix_g"), ("conv_b", "conv_b"), ("conv_ng", "conv_norm_g"), ("conv_nb", "conv_norm_b"),
                      ("b_conv_out", "b_conv_out"), ("g_ffn", "norm_ffn_g"), ("g_final", "norm_final_g")):
        put(1, name, vec(z[key]))
    put(1, "conv_w", z["conv_w"].reshape(TAPS, KT, P).transpose(2, 1, 0).reshape(P, KT * TAPS))
    put(1, "cmp_pos", z["cmp_k_pos"].reshape(16, P).T)
    put(1, "cmp_pos", z["cmp_v_pos"].reshape(16, P).T, 16)
    for name in ("ln_in_g", "ln_in_b", "pool_scale", "ln1_g", "ln1_b", "ln2_g", "ln2_b"):
        put(2, name, vec(z[name + "_2"]))
    put(2, "conv_w", z["conv_w_2"].reshape(4, 24, P).transpose(2, 1, 0).reshape(P, 96))
    put(2, "a_log", np.broadcast_to(z["a_log_2"].reshape(1, 8), (P, 8)))
    put(2, "dt_bias", np.broadcast_to(z["dt_bias_2"].reshape(1, 8), (P, 8)))
    put(2, "o_norm", vec(z["o_norm_w_2"]))
    for name in ("g_mix", "g_mlp", "g_pe", "g_final"):
        put(3, name, vec(z[name + "_3"]))
    put(3, "sinks", np.broadcast_to(z["sinks_3"].reshape(1, 8), (P, 8)))
    return c


def arrays_of(z, blocks=(1, 2, 3)):
    w2 = z["cmp_k_w2"].reshape(2, P, DH).transpose(1, 0, 2)
    parts = [u for b in blocks for u in {1: stream_1, 2: stream_2, 3: stream_3}[b](z)]
    n = plan(blocks)[3] - sum(len(u) for u in parts)

    def features_first(a):
        return np.ascontiguousarray(a.reshape(S, -1, P).transpose(2, 1, 0))

    return {
        "w": np.concatenate(parts + [np.zeros((n, P, KT * P), np.float32)]),
        "cols": columns(z),
        "consts": constants(),
        "x": features_first(z["x"]),
        "p2": features_first(z["p_2"]),
        "p3": features_first(z["p_3"]),
        "pos": np.ascontiguousarray(np.broadcast_to(z["positions"].reshape(1, S), (P, S))),
        "cw2k": np.ascontiguousarray(np.concatenate([w2, w2], 2)),
        "cw2v": np.ascontiguousarray(z["cmp_v_w2"].reshape(2, P, DH).transpose(1, 0, 2)),
        "rel": np.ascontiguousarray(z["rel_bias_3"]),
        "bucket": bucket_of_distance(),
    }


def bucket_of_distance():
    dist = 255 - np.arange(384)
    safe = np.maximum(dist, 1).astype(np.float32)
    large = 16 + (np.log(safe / np.float32(16)) / np.float32(math.log(8)) * np.float32(16)).astype(np.int32)
    b = np.where(dist < 16, np.maximum(dist, 0), np.minimum(large, 31))
    inside = (dist >= 0) & (dist < 128)
    return np.concatenate([(np.arange(32)[:, None] == b[None, :]) & inside[None], ~inside[None]]).astype(np.float32)


def kernel(**inputs):
    import concourse.bacc as bacc
    from concourse.bass_utils import run_bass_kernel_spmd

    nc = bacc.Bacc("TRN2", target_bir_lowering=False, num_devices=1)
    arrays = {f"in_{k}_dram": a for k, a in arrays_of({k: np.asarray(v) for k, v in inputs.items()}).items()}
    t = {k[3:-5]: nc.dram_tensor(k, a.shape, mybir.dt.from_np(a.dtype), kind="ExternalInput").ap() for k, a in arrays.items()}
    out = nc.dram_tensor("out_0_dram", (P, KT, S), F32, kind="ExternalOutput").ap()
    build(nc, t, out)
    got = run_bass_kernel_spmd(nc, [arrays], core_ids=[0]).results[0]["out_0_dram"]
    return np.ascontiguousarray(got.transpose(2, 1, 0)).reshape(1, S, D)
```
